# Optimizing a Trainium2 kernel written in Bass

```python
import math
import jax, jax.numpy as jnp
from jax import lax
import numpy as np

D_MODEL = 1024
BATCH = 1
SEQ = 256
DEPTH = 2

N_MIXERS = 2
N_SB_LAYERS = (DEPTH + 1) // 2
N_MLA_LAYERS = DEPTH // 2
Q_BLOCK = 128
EPS = 1e-6

SB_HEADS = 16
SB_HEAD_DIM = D_MODEL // SB_HEADS

MLA_HEADS = 16
MLA_Q_LORA = 256
MLA_KV_LORA = 128
MLA_NOPE_DIM = 64
MLA_ROPE_DIM = 32
MLA_V_DIM = 64
ROPE_THETA = 10000.0

D_FF = 2816
FFN_RESIDUAL_WEIGHT = 0.5
N_NORMS_PER_LAYER = 6


def rms_norm(x, g):
    xf = x.astype(jnp.float32)
    y = xf * lax.rsqrt(jnp.mean(xf * xf, axis=-1, keepdims=True) + EPS)
    return (y * g.astype(jnp.float32)).astype(x.dtype)

def swiglu(x, w_in, w_out):
    gate, up = jnp.split(x @ w_in, 2, axis=-1)
    return (jax.nn.silu(gate) * up) @ w_out

def apply_rope(x, positions):
    d = x.shape[-1]
    inv_freq = ROPE_THETA ** (-jnp.arange(0, d, 2, dtype=jnp.float32) / d)
    ang = positions.astype(jnp.float32)[..., None] * inv_freq
    cos = jnp.cos(ang)[:, :, None, :].astype(x.dtype)
    sin = jnp.sin(ang)[:, :, None, :].astype(x.dtype)
    x1, x2 = jnp.split(x, 2, axis=-1)
    return jnp.concatenate([x1 * cos - x2 * sin, x2 * cos + x1 * sin], axis=-1)

def query_blocks(q):
    b, s, h, d = q.shape
    return q.reshape(b, s // Q_BLOCK, Q_BLOCK, h, d).transpose(1, 0, 2, 3, 4)

def merge_blocks(o):
    nb, b, qb, h, dv = o.shape
    return o.transpose(1, 0, 2, 3, 4).reshape(b, nb * qb, h * dv)

def stick_breaking_attention(h, w_in, w_out):
    b, s, _ = h.shape
    qkv = (h @ w_in).reshape(b, s, 3, SB_HEADS, SB_HEAD_DIM)
    q, k, v = qkv[:, :, 0], qkv[:, :, 1], qkv[:, :, 2]
    scale = 1.0 / math.sqrt(SB_HEAD_DIM)
    k_idx = jnp.arange(s)

    def block(args):
        qb, bi = args
        q_idx = bi * Q_BLOCK + jnp.arange(Q_BLOCK)
        z = jnp.einsum('bqhd,bkhd->bhqk', qb, k).astype(jnp.float32) * scale
        mask = k_idx[None, :] < q_idx[:, None]
        sp = jnp.where(mask, jax.nn.softplus(z), 0.0)
        tail = lax.cumsum(sp, axis=sp.ndim - 1, reverse=True) - sp
        log_a = jax.nn.log_sigmoid(z) - tail
        a = jnp.where(mask, jnp.exp(log_a), 0.0).astype(v.dtype)
        return jnp.einsum('bhqk,bkhd->bqhd', a, v)

    nb = s // Q_BLOCK
    o = lax.map(block, (query_blocks(q), jnp.arange(nb)))
    return merge_blocks(o) @ w_out

def multi_head_latent_attention(h, positions, w_in, q_norm, w_uq, kv_norm, w_ukv, w_out):
    b, s, _ = h.shape
    proj = h @ w_in
    c_q = proj[..., :MLA_Q_LORA]
    c_kv = proj[..., MLA_Q_LORA:MLA_Q_LORA + MLA_KV_LORA]
    k_rope = proj[..., MLA_Q_LORA + MLA_KV_LORA:][:, :, None, :]
    k_rope = apply_rope(k_rope, positions)[:, :, 0, :]

    q = (rms_norm(c_q, q_norm) @ w_uq).reshape(b, s, MLA_HEADS, MLA_NOPE_DIM + MLA_ROPE_DIM)
    q_nope = q[..., :MLA_NOPE_DIM]
    q_rope = apply_rope(q[..., MLA_NOPE_DIM:], positions)
    q = jnp.concatenate([q_nope, q_rope], axis=-1)

    kv = (rms_norm(c_kv, kv_norm) @ w_ukv).reshape(b, s, MLA_HEADS, MLA_NOPE_DIM + MLA_V_DIM)
    k_nope = kv[..., :MLA_NOPE_DIM]
    v = kv[..., MLA_NOPE_DIM:]
    scale = 1.0 / math.sqrt(MLA_NOPE_DIM + MLA_ROPE_DIM)
    k_idx = jnp.arange(s)

    def block(args):
        qb, bi = args
        q_idx = bi * Q_BLOCK + jnp.arange(Q_BLOCK)
        qn, qr = qb[..., :MLA_NOPE_DIM], qb[..., MLA_NOPE_DIM:]
        scores = (jnp.einsum('bqhd,bkhd->bhqk', qn, k_nope)
                  + jnp.einsum('bqhr,bkr->bhqk', qr, k_rope)).astype(jnp.float32) * scale
        mask = k_idx[None, :] <= q_idx[:, None]
        scores = jnp.where(mask, scores, -jnp.inf)
        p = jax.nn.softmax(scores, axis=-1).astype(v.dtype)
        return jnp.einsum('bhqk,bkhd->bqhd', p, v)

    nb = s // Q_BLOCK
    o = lax.map(block, (query_blocks(q), jnp.arange(nb)))
    return merge_blocks(o) @ w_out

def first_inputs(seed: int = 0) -> dict:
    key = jax.random.key(seed)
    ks = jax.random.split(key, 16)

    def w(k, shape, fan_in):
        return jax.random.normal(k, shape, jnp.float32) * fan_in ** -0.5

    def gain(k, shape):
        return 1.0 + 0.05 * jax.random.normal(k, shape, jnp.float32)

    sb_width = SB_HEADS * SB_HEAD_DIM
    mla_in = MLA_Q_LORA + MLA_KV_LORA + MLA_ROPE_DIM
    return {
        "x": jax.random.normal(ks[0], (BATCH, SEQ, D_MODEL), jnp.float32),
        "positions": jnp.broadcast_to(jnp.arange(SEQ, dtype=jnp.int32)[None, :], (BATCH, SEQ)),
        "norm_g": gain(ks[1], (DEPTH, N_NORMS_PER_LAYER, D_MODEL)),
        "ffn_w_in": w(ks[2], (DEPTH, 2, D_MODEL, 2 * D_FF), D_MODEL),
        "ffn_w_out": w(ks[3], (DEPTH, 2, D_FF, D_MODEL), D_FF),
        "sb_w_in": w(ks[4], (N_SB_LAYERS, D_MODEL, 3 * sb_width), D_MODEL),
        "sb_w_out": w(ks[5], (N_SB_LAYERS, sb_width, D_MODEL), sb_width),
        "mla_w_in": w(ks[6], (N_MLA_LAYERS, D_MODEL, mla_in), D_MODEL),
        "mla_q_norm": gain(ks[7], (N_MLA_LAYERS, MLA_Q_LORA)),
        "mla_w_uq": w(ks[8], (N_MLA_LAYERS, MLA_Q_LORA, MLA_HEADS * (MLA_NOPE_DIM + MLA_ROPE_DIM)), MLA_Q_LORA),
        "mla_kv_norm": gain(ks[9], (N_MLA_LAYERS, MLA_KV_LORA)),
        "mla_w_ukv": w(ks[10], (N_MLA_LAYERS, MLA_KV_LORA, MLA_HEADS * (MLA_NOPE_DIM + MLA_V_DIM)), MLA_KV_LORA),
        "mla_w_out": w(ks[11], (N_MLA_LAYERS, MLA_HEADS * MLA_V_DIM, D_MODEL), MLA_HEADS * MLA_V_DIM),
    }

def first_block(x, positions, norm_g, ffn_w_in, ffn_w_out, sb_w_in, sb_w_out,
              mla_w_in, mla_q_norm, mla_w_uq, mla_kv_norm, mla_w_ukv, mla_w_out):
    for i in range(DEPTH):
        g = norm_g[i]
        f = swiglu(rms_norm(x, g[0]), ffn_w_in[i, 0], ffn_w_out[i, 0])
        x = x + FFN_RESIDUAL_WEIGHT * rms_norm(f, g[1])
        h = rms_norm(x, g[2])
        j = i // N_MIXERS
        if i % N_MIXERS == 0:
            m = stick_breaking_attention(h, sb_w_in[j], sb_w_out[j])
        else:
            m = multi_head_latent_attention(h, positions, mla_w_in[j], mla_q_norm[j], mla_w_uq[j],
                                            mla_kv_norm[j], mla_w_ukv[j], mla_w_out[j])
        x = x + rms_norm(m, g[3])
        f = swiglu(rms_norm(x, g[4]), ffn_w_in[i, 1], ffn_w_out[i, 1])
        x = x + FFN_RESIDUAL_WEIGHT * rms_norm(f, g[5])
    return x


N_A_LAYERS = DEPTH // 2
N_B_LAYERS = DEPTH - N_A_LAYERS
PLE_DIM = 256
NORM_EPS = 1e-6
GATED_NORM_EPS = 1e-5
SSM_EXPAND = 2
D_INNER = SSM_EXPAND * D_MODEL
SSM_HEADDIM = 64
SSM_HEADS = D_INNER // SSM_HEADDIM
SSM_GROUPS = 8
SSM_HPG = SSM_HEADS // SSM_GROUPS
SSM_STATE = 128
CONV_K = 4
CONV_DIM = D_INNER + 2 * SSM_GROUPS * SSM_STATE
D_IN_PROJ = D_INNER + CONV_DIM + SSM_HEADS
SSD_CHUNK = 128
HEAD_DIM = 64
N_Q_HEADS = D_MODEL // HEAD_DIM
N_KV_HEADS = 2
Q_PER_KV = N_Q_HEADS // N_KV_HEADS
WINDOW = 128
ROT_DIM = HEAD_DIM // 4
ROPE_THETA_2 = 500000.0
KV_DIM = N_KV_HEADS * HEAD_DIM
PEER_HEADS = 8
N_KEYS = 128
N_EXPERTS = N_KEYS * N_KEYS
PEER_DK = 256
PEER_HALF = PEER_DK // 2
PEER_TOPK = 16
PEER_BLOCK = 128


def rmsnorm(x, g, eps=NORM_EPS):
    xf = x.astype(jnp.float32)
    xf = xf * lax.rsqrt(jnp.mean(xf * xf, axis=-1, keepdims=True) + eps)
    return (xf * g.astype(jnp.float32)).astype(x.dtype)

def rope_tables(positions):
    inv = jnp.power(ROPE_THETA_2, -jnp.arange(0, ROT_DIM, 2, dtype=jnp.float32) / ROT_DIM)
    ang = positions.astype(jnp.float32)[..., None] * inv
    return jnp.cos(ang)[:, :, None, :], jnp.sin(ang)[:, :, None, :]

def apply_partial_rope(t, cos, sin):
    half = ROT_DIM // 2
    t1 = t[..., :half].astype(jnp.float32)
    t2 = t[..., half:ROT_DIM].astype(jnp.float32)
    rot = jnp.concatenate([t1 * cos - t2 * sin, t2 * cos + t1 * sin], axis=-1).astype(t.dtype)
    return jnp.concatenate([rot, t[..., ROT_DIM:]], axis=-1)

def causal_conv(u, w, b):
    S = u.shape[1]
    up = jnp.pad(u, ((0, 0), (CONV_K - 1, 0), (0, 0)))
    out = b
    for k in range(CONV_K):
        out = out + up[:, k:k + S] * w[k]
    return out

def ssd_chunked(xs, dt, A, Bm, Cm):
    Bsz, S = xs.shape[0], xs.shape[1]
    nc = S // SSD_CHUNK
    f32 = jnp.float32
    X = (xs.astype(f32) * dt[..., None]).reshape(Bsz, nc, SSD_CHUNK, SSM_GROUPS, SSM_HPG, SSM_HEADDIM)
    a = (dt * A).reshape(Bsz, nc, SSD_CHUNK, SSM_GROUPS, SSM_HPG)
    Bc = Bm.astype(f32).reshape(Bsz, nc, SSD_CHUNK, SSM_GROUPS, SSM_STATE)
    Cc = Cm.astype(f32).reshape(Bsz, nc, SSD_CHUNK, SSM_GROUPS, SSM_STATE)
    a_cs = jnp.cumsum(a, axis=2)
    causal = jnp.tril(jnp.ones((SSD_CHUNK, SSD_CHUNK), dtype=bool))[:, :, None, None]
    seg = a_cs[:, :, :, None] - a_cs[:, :, None, :]
    L = jnp.exp(jnp.where(causal, seg, -jnp.inf))
    cb = jnp.einsum('bclgn,bcsgn->bclsg', Cc, Bc)
    y_diag = jnp.einsum('bclsg,bclsgr,bcsgrp->bclgrp', cb, L, X)
    decay_to_end = jnp.exp(a_cs[:, :, -1:] - a_cs)
    states = jnp.einsum('bclgn,bclgr,bclgrp->bcgrpn', Bc, decay_to_end, X)
    chunk_decay = jnp.exp(a_cs[:, :, -1])

    def step(h, inp):
        st, dc = inp
        return h * dc[..., None, None] + st, h

    h0 = jnp.zeros((Bsz, SSM_GROUPS, SSM_HPG, SSM_HEADDIM, SSM_STATE), f32)
    _, prev = lax.scan(step, h0, (jnp.moveaxis(states, 1, 0), jnp.moveaxis(chunk_decay, 1, 0)))
    prev = jnp.moveaxis(prev, 0, 1)
    y_off = jnp.einsum('bclgn,bcgrpn,bclgr->bclgrp', Cc, prev, jnp.exp(a_cs))
    return (y_diag + y_off).reshape(Bsz, S, SSM_HEADS, SSM_HEADDIM)

def mamba2_mixer(x, norm_g, in_w, conv_w, conv_b, dt_bias, A_log, D_skip, gate_norm, out_w):
    Bsz, S, _ = x.shape
    f32 = jnp.float32
    h = rmsnorm(x, norm_g)
    zxbcdt = h @ in_w
    z = zxbcdt[..., :D_INNER]
    xbc = zxbcdt[..., D_INNER:D_INNER + CONV_DIM]
    dt_raw = zxbcdt[..., D_INNER + CONV_DIM:]
    xbc = jax.nn.silu(causal_conv(xbc, conv_w, conv_b))
    gn = SSM_GROUPS * SSM_STATE
    xs = xbc[..., :D_INNER].reshape(Bsz, S, SSM_HEADS, SSM_HEADDIM)
    Bm = xbc[..., D_INNER:D_INNER + gn].reshape(Bsz, S, SSM_GROUPS, SSM_STATE)
    Cm = xbc[..., D_INNER + gn:].reshape(Bsz, S, SSM_GROUPS, SSM_STATE)
    dt = jax.nn.softplus(dt_raw.astype(f32) + dt_bias.astype(f32))
    A = -jnp.exp(A_log.astype(f32))
    y = ssd_chunked(xs, dt, A, Bm, Cm)
    y = y + xs.astype(f32) * D_skip.astype(f32)[:, None]
    y = y.reshape(Bsz, S, D_INNER) * jax.nn.silu(z.astype(f32))
    y = y.reshape(Bsz, S, SSM_GROUPS, D_INNER // SSM_GROUPS)
    y = y * lax.rsqrt(jnp.mean(y * y, axis=-1, keepdims=True) + GATED_NORM_EPS)
    y = (y.reshape(Bsz, S, D_INNER) * gate_norm.astype(f32)).astype(x.dtype)
    return y @ out_w

def shared_kv(x, norm_g, kv_w, kv_b, cos, sin):
    Bsz, S, _ = x.shape
    kv = rmsnorm(x, norm_g) @ kv_w + kv_b
    k = kv[..., :KV_DIM].reshape(Bsz, S, N_KV_HEADS, HEAD_DIM)
    v = kv[..., KV_DIM:].reshape(Bsz, S, N_KV_HEADS, HEAD_DIM)
    return apply_partial_rope(k, cos, sin), v

def swa_sink_attention(x, norm_g, q_w, q_b, sinks, o_w, o_b, k, v, cos, sin):
    Bsz, S, _ = x.shape
    nb = S // WINDOW
    f32 = jnp.float32
    h = rmsnorm(x, norm_g)
    q = (h @ q_w + q_b).reshape(Bsz, S, N_Q_HEADS, HEAD_DIM)
    q = apply_partial_rope(q, cos, sin)
    qb = q.reshape(Bsz, nb, WINDOW, N_KV_HEADS, Q_PER_KV, HEAD_DIM)

    def band(t):
        tp = jnp.concatenate([jnp.zeros_like(t[:, :WINDOW]), t], axis=1)
        tp = tp.reshape(Bsz, nb + 1, WINDOW, N_KV_HEADS, HEAD_DIM)
        return jnp.concatenate([tp[:, :-1], tp[:, 1:]], axis=2)

    kb, vb = band(k), band(v)
    sink_logits = sinks.astype(f32).reshape(N_KV_HEADS, Q_PER_KV)
    qi = jnp.arange(WINDOW)[:, None]
    kj = jnp.arange(2 * WINDOW)[None, :]
    in_window = (kj > qi) & (kj <= qi + WINDOW)
    scale = HEAD_DIM ** -0.5

    def block(inp):
        qblk, kblk, vblk, n = inp
        s = jnp.einsum('bqgrd,bkgd->bgrqk', qblk, kblk).astype(f32) * scale
        valid = in_window & (n * WINDOW - WINDOW + kj >= 0)
        s = jnp.where(valid, s, -jnp.inf)
        sink = jnp.broadcast_to(sink_logits[None, :, :, None, None], s.shape[:-1] + (1,))
        pr = jax.nn.softmax(jnp.concatenate([s, sink], axis=-1), axis=-1)[..., :-1]
        return jnp.einsum('bgrqk,bkgd->bqgrd', pr.astype(vblk.dtype), vblk)

    o = lax.map(block, (jnp.moveaxis(qb, 1, 0), jnp.moveaxis(kb, 1, 0), jnp.moveaxis(vb, 1, 0),
                        jnp.arange(nb)))
    o = jnp.moveaxis(o, 0, 1).reshape(Bsz, S, N_Q_HEADS * HEAD_DIM)
    return o @ o_w + o_b

def peer_ffn(x, norm_g, q_w, sub_keys, u, v):
    Bsz, S, D = x.shape
    T = Bsz * S
    h = rmsnorm(x, norm_g).reshape(T, D)
    q = (h @ q_w).reshape(T, PEER_HEADS, 2, PEER_HALF)
    s = jnp.einsum('thcd,ckd->thck', q, sub_keys).astype(jnp.float32)
    s1, i1 = lax.top_k(s[:, :, 0], PEER_TOPK)
    s2, i2 = lax.top_k(s[:, :, 1], PEER_TOPK)
    cand_s = (s1[..., :, None] + s2[..., None, :]).reshape(T, PEER_HEADS, PEER_TOPK * PEER_TOPK)
    cand_i = (i1[..., :, None] * N_KEYS + i2[..., None, :]).reshape(T, PEER_HEADS, PEER_TOPK * PEER_TOPK)
    best_s, best_pos = lax.top_k(cand_s, PEER_TOPK)
    idx = jnp.take_along_axis(cand_i, best_pos, axis=-1)
    gate = jax.nn.softmax(best_s, axis=-1).astype(x.dtype)
    nblk = T // PEER_BLOCK

    def block(inp):
        hb, ib, gb = inp
        a = jnp.einsum('nd,nhkd->nhk', hb, u[ib])
        w = gb * jax.nn.gelu(a, approximate=False)
        return jnp.einsum('nhk,nhkd->nd', w, v[ib])

    out = lax.map(block, (h.reshape(nblk, PEER_BLOCK, D),
                          idx.reshape(nblk, PEER_BLOCK, PEER_HEADS, PEER_TOPK),
                          gate.reshape(nblk, PEER_BLOCK, PEER_HEADS, PEER_TOPK)))
    return out.reshape(Bsz, S, D)

def ple_add(x, p_i, norm_g, proj, gate_w):
    gate = jax.nn.sigmoid(rmsnorm(x, norm_g) @ gate_w)
    return x + (p_i @ proj) * gate

def second_inputs(seed: int = 0) -> dict:
    key = jax.random.key(seed)
    ks = jax.random.split(key, 32)
    f32 = jnp.float32

    def nrm(k, shape, scale):
        return jax.random.normal(k, shape, f32) * scale

    def gain(k, shape):
        return 1.0 + 0.05 * jax.random.normal(k, shape, f32)

    dt0 = jnp.exp(jax.random.uniform(ks[6], (N_A_LAYERS, SSM_HEADS), f32,
                                     minval=math.log(1e-3), maxval=math.log(1e-1)))
    inp = {
        'x': nrm(ks[0], (BATCH, SEQ, D_MODEL), 1.0),
        'p': nrm(ks[1], (DEPTH, BATCH, SEQ, PLE_DIM), 1.0),
        'positions': jnp.arange(SEQ, dtype=jnp.int32)[None, :]
                     + jax.random.randint(ks[2], (BATCH, 1), 0, 4096, dtype=jnp.int32),
        'ssm_norm': gain(ks[3], (N_A_LAYERS, D_MODEL)),
        'ssm_in_w': nrm(ks[4], (N_A_LAYERS, D_MODEL, D_IN_PROJ), D_MODEL ** -0.5),
        'ssm_conv_w': nrm(ks[5], (N_A_LAYERS, CONV_K, CONV_DIM), CONV_K ** -0.5),
        'ssm_conv_b': nrm(ks[7], (N_A_LAYERS, CONV_DIM), 0.02),
        'ssm_dt_bias': dt0 + jnp.log(-jnp.expm1(-dt0)),
        'ssm_A_log': jnp.log(jax.random.uniform(ks[8], (N_A_LAYERS, SSM_HEADS), f32, minval=1.0, maxval=16.0)),
        'ssm_D': gain(ks[9], (N_A_LAYERS, SSM_HEADS)),
        'ssm_gate_norm': gain(ks[10], (N_A_LAYERS, D_INNER)),
        'ssm_out_w': nrm(ks[11], (N_A_LAYERS, D_INNER, D_MODEL), D_INNER ** -0.5),
        'kv_norm': gain(ks[12], (D_MODEL,)),
        'kv_w': nrm(ks[13], (D_MODEL, 2 * KV_DIM), D_MODEL ** -0.5),
        'kv_b': nrm(ks[14], (2 * KV_DIM,), 0.02),
        'attn_norm': gain(ks[15], (N_B_LAYERS, D_MODEL)),
        'q_w': nrm(ks[16], (N_B_LAYERS, D_MODEL, N_Q_HEADS * HEAD_DIM), D_MODEL ** -0.5),
        'q_b': nrm(ks[17], (N_B_LAYERS, N_Q_HEADS * HEAD_DIM), 0.02),
        'sinks': nrm(ks[18], (N_B_LAYERS, N_Q_HEADS), 0.5),
        'o_w': nrm(ks[19], (N_B_LAYERS, N_Q_HEADS * HEAD_DIM, D_MODEL), (N_Q_HEADS * HEAD_DIM) ** -0.5),
        'o_b': nrm(ks[20], (N_B_LAYERS, D_MODEL), 0.02),
        'peer_norm': gain(ks[21], (DEPTH, D_MODEL)),
        'peer_q_w': nrm(ks[22], (DEPTH, D_MODEL, PEER_HEADS * PEER_DK), D_MODEL ** -0.5),
        'peer_sub_keys': nrm(ks[23], (DEPTH, 2, N_KEYS, PEER_HALF), PEER_HALF ** -0.5),
        'peer_u': nrm(ks[24], (DEPTH, N_EXPERTS, D_MODEL), D_MODEL ** -0.5),
        'peer_v': nrm(ks[25], (DEPTH, N_EXPERTS, D_MODEL), PEER_HEADS ** -0.5),
        'ple_norm': gain(ks[26], (DEPTH, D_MODEL)),
        'ple_proj': nrm(ks[27], (DEPTH, PLE_DIM, D_MODEL), PLE_DIM ** -0.5),
        'ple_gate_w': nrm(ks[28], (DEPTH, D_MODEL, D_MODEL), D_MODEL ** -0.5),
        'final_norm': gain(ks[29], (D_MODEL,)),
    }
    return inp

def second_block(x, p, positions, ssm_norm, ssm_in_w, ssm_conv_w, ssm_conv_b, ssm_dt_bias, ssm_A_log,
              ssm_D, ssm_gate_norm, ssm_out_w, kv_norm, kv_w, kv_b, attn_norm, q_w, q_b, sinks,
              o_w, o_b, peer_norm, peer_q_w, peer_sub_keys, peer_u, peer_v, ple_norm, ple_proj,
              ple_gate_w, final_norm):
    cos, sin = rope_tables(positions)
    k_shared, v_shared = None, None
    for i in range(DEPTH):
        if i < N_A_LAYERS:
            j = i
            x = x + mamba2_mixer(x, ssm_norm[j], ssm_in_w[j], ssm_conv_w[j], ssm_conv_b[j],
                                 ssm_dt_bias[j], ssm_A_log[j], ssm_D[j], ssm_gate_norm[j], ssm_out_w[j])
        else:
            j = i - N_A_LAYERS
            x = x + swa_sink_attention(x, attn_norm[j], q_w[j], q_b[j], sinks[j], o_w[j], o_b[j],
                                       k_shared, v_shared, cos, sin)
        x = x + peer_ffn(x, peer_norm[i], peer_q_w[i], peer_sub_keys[i], peer_u[i], peer_v[i])
        x = ple_add(x, p[i], ple_norm[i], ple_proj[i], ple_gate_w[i])
        if i == N_A_LAYERS - 1:
            k_shared, v_shared = shared_kv(x, kv_norm, kv_w, kv_b, cos, sin)
    return rmsnorm(x, final_norm)


def setup_inputs(seed=0):
    out = dict(first_inputs(seed))
    for name, value in second_inputs(seed + 1).items():
        if name != "x":
            out[name + "_2"] = value
    return out


def reference(
    x, positions, norm_g, ffn_w_in, ffn_w_out, sb_w_in, sb_w_out, mla_w_in, mla_q_norm,
    mla_w_uq, mla_kv_norm, mla_w_ukv, mla_w_out, p_2, positions_2, ssm_norm_2, ssm_in_w_2,
    ssm_conv_w_2, ssm_conv_b_2, ssm_dt_bias_2, ssm_A_log_2, ssm_D_2, ssm_gate_norm_2,
    ssm_out_w_2, kv_norm_2, kv_w_2, kv_b_2, attn_norm_2, q_w_2, q_b_2, sinks_2, o_w_2, o_b_2,
    peer_norm_2, peer_q_w_2, peer_sub_keys_2, peer_u_2, peer_v_2, ple_norm_2, ple_proj_2,
    ple_gate_w_2, final_norm_2,
):
    x = first_block(
        x, positions, norm_g, ffn_w_in, ffn_w_out, sb_w_in, sb_w_out, mla_w_in, mla_q_norm,
        mla_w_uq, mla_kv_norm, mla_w_ukv, mla_w_out,
    )
    return second_block(
        x, p_2, positions_2, ssm_norm_2, ssm_in_w_2, ssm_conv_w_2, ssm_conv_b_2, ssm_dt_bias_2,
        ssm_A_log_2, ssm_D_2, ssm_gate_norm_2, ssm_out_w_2, kv_norm_2, kv_w_2, kv_b_2,
        attn_norm_2, q_w_2, q_b_2, sinks_2, o_w_2, o_b_2, peer_norm_2, peer_q_w_2,
        peer_sub_keys_2, peer_u_2, peer_v_2, ple_norm_2, ple_proj_2, ple_gate_w_2, final_norm_2,
    )


_drawn_inputs = setup_inputs


def setup_inputs(seed=0):
    import zlib

    import numpy as np

    out = dict(_drawn_inputs(seed))
    spreads = {}
    factors = {'ssm_conv_b_2': 3.175,
     'ssm_D_2': 2.99,
     'kv_norm_2': 5.363,
     'kv_b_2': 5.688,
     'attn_norm_2': 8.0,
     'q_b_2': 8.0,
     'sinks_2': 8.0,
     'o_b_2': 15.421,
     'ple_norm_2': 6.93}
    for name, (base, spread) in spreads.items():
        noise = np.random.default_rng([zlib.crc32(name.encode()), seed]).standard_normal(out[name].shape)
        drawn = base * np.exp(spread * noise) if base else spread * noise
        out[name] = __import__('jax').numpy.asarray(drawn.astype(out[name].dtype))
    for name, factor in factors.items():
        out[name] = (out[name] * factor).astype(out[name].dtype)
    return out
```

```python
import concourse.bass as bass
from concourse import mybir
from contextlib import ExitStack
import numpy as np

F32 = mybir.dt.float32
U32 = mybir.dt.uint32
I32 = mybir.dt.int32
ACT = mybir.ActivationFunctionType
ALU = mybir.AluOpType
AX = mybir.AxisListType

P = 128
D = 1024
T = 256
TB = T // P
KD = D // P
FF = 2816
FC = FF // P
HEADS = 16
QL, KVL, ROPE, NOPE = 256, 128, 32, 64
MLA_IN = QL + KVL + ROPE
QD = NOPE + ROPE
DI = 2048
SH, SG, SN, SP_ = 32, 8, 128, 64
HPG = SH // SG
CONV_TILES = (DI + 2 * SG * SN) // P
KEYS = 128
TOPK = 16
PH = 8
SUBS = 2 * PH
ROT = 16
NEG = -1.0e30
EPS = 1e-6

BLK = 1024
RING = 4
LAYERS = ["ffn0", "sb", "ffn1", "ffn2", "mla", "ffn3", "ssm", "peer0", "ple0", "swa", "peer1", "ple1"]
PARTS = [("ffn0", 3 * FC), ("sb_qkv", 24), ("sb_out", 8), ("ffn1", 3 * FC), ("ffn2", 3 * FC),
         ("mla_in", 4), ("mla_uq", 3), ("mla_ukv", 2), ("mla_out", 8), ("ffn3", 3 * FC),
         ("ssm_z", 16), ("ssm_xbc", CONV_TILES), ("ssm_dt", 1), ("ssm_out", 16),
         ("peer0_q", SUBS), ("peer0_u", KEYS), ("peer0_v", KEYS), ("ple0_gate", 8), ("ple0_proj", 2),
         ("swa_kv", 2), ("swa_q", 8), ("swa_out", 8),
         ("peer1_q", SUBS), ("peer1_u", KEYS), ("peer1_v", KEYS), ("ple1_gate", 8), ("ple1_proj", 2)]


def first_blocks():
    at, n = {}, 0
    for name, count in PARTS:
        at[name] = n
        n += count
    at["end"] = n
    return at


AT = first_blocks()

COLS = [("ident", P), ("up_incl", P), ("lo_incl", P), ("up_strict", P), ("neg_strict", P),
        ("neg_causal", 3 * P), ("neg_window", 3 * P), ("neg_after", P), ("ones", P), ("iota", P),
        ("inv", 24), ("nhalf", 16), ("gains", 13 * KD), ("gate_norm", DI // P), ("q_norm", 2), ("kv_norm", 1),
        ("conv", CONV_TILES * 5), ("subkeys", 2 * 2 * KEYS), ("dt_bias", SH), ("a_log", SH), ("d_skip", SH),
        ("sinks", HEADS), ("kv_b", 256), ("pT", 2 * 2 * T)]


def col_offsets():
    at, n = {}, 0
    for name, width in COLS:
        at[name] = (n, width)
        n += width
    at["end"] = (n, 0)
    return at


CAT = col_offsets()
NCOLS = CAT["end"][0]
ROWS = 9

NORM_OF = {"ffn0": 0, "sb": 1, "ffn1": 2, "ffn2": 3, "mla": 4, "ffn3": 5, "ssm": 6, "peer0": 7, "ple0": 8,
           "kv": 9, "swa": 10, "peer1": 11, "ple1": 12}


def build_program(nc, stream, x_in, pos_in, cols_in, rows_in, out, stop=len(LAYERS)):
    layers = LAYERS[:stop]
    n_blocks = AT["end"] if stop == len(LAYERS) else AT[
        {"ffn0": "sb_qkv", "sb": "ffn1", "ffn1": "ffn2", "ffn2": "mla_in", "mla": "ffn3", "ffn3": "ssm_z",
         "ssm": "peer0_q", "peer0": "ple0_gate", "ple0": "swa_kv", "swa": "peer1_q",
         "peer1": "ple1_gate"}[layers[-1]]]
    ctx = ExitStack()
    with ctx:
        def sb(name, shape, dt=F32):
            return ctx.enter_context(nc.sbuf_tensor(name, shape, dt))

        def sem(name):
            return ctx.enter_context(nc.semaphore(name))

        x = sb("x", [P, TB, D])
        hT = sb("hT", [P, KD, T])
        ring = sb("ring", [P, RING, BLK])
        cols = sb("cols", [P, NCOLS])
        row = sb("row", [P, 2, D])
        arena = sb("arena", [P, KEYS * T])
        pick = sb("pick", [P, 3, T])
        ss = sb("ss", [P, 16])
        ms = sb("ms", [P, 16])
        rs = sb("rs", [P, 16])
        pos = sb("pos", [P, 2 * TB], I32)
        posf = sb("posf", [P, 2 * TB])
        ang = sb("ang", [P, 4, TB, 24])
        cosT = sb("cosT", [P, TB, 24])
        sinT = sb("sinT", [P, TB, 24])
        ps = ctx.enter_context(nc.psum_tensor("ps", [P, 8, 512], F32))

        def col(name, *dims):
            o, w = CAT[name]
            a = cols[:, o:o + w]
            return split(a, *dims) if dims else a

        def split(a, *dims):
            if len(dims) == 1:
                return a
            names = "abcd"[:len(dims)]
            return a.rearrange(f"p ({' '.join(names)}) -> p {' '.join(names)}",
                               **{n: d for n, d in zip(names[1:], dims[1:])})

        def region(at, *dims):
            n = 1
            for d in dims:
                n *= d
            return split(arena[:, at:at + n], *dims), at + n

        def gain(v, k):
            o = CAT["gains"][0] + v * KD + k
            return cols[:, o:o + 1]

        loaded = [sem(f"block_loaded{i}") for i in range(RING)]
        used = sem("blocks_used")
        x_loaded, cols_loaded, pos_loaded = sem("x_loaded"), sem("cols_loaded"), sem("pos_loaded")
        row_loaded = [sem("row_loaded0"), sem("row_loaded1")]
        x_ready = sem("x_ready")
        ss_ready, ms_ready, rs_ready = sem("ss_ready"), sem("ms_ready"), sem("rs_ready")
        xn_ready = sem("xn_ready")
        xT_ready = sem("xT_ready")
        hT_a, hT_d = sem("hT_by_act"), sem("hT_by_dve")
        silu_ready, hidden_ready = sem("silu_ready"), sem("hidden_ready")
        dve_chain, act_chain = sem("dve_chain"), sem("act_chain")
        out_done = sem("out_done")
        xn, _ = region(0, TB, D)
        ARENA = TB * D
        S = {}

        def of(name):
            if name not in S:
                S[name] = sem(name)
            return S[name]

        n_stats = [0]

        def sb_regions():
            r, at = {}, ARENA
            for name, dims in (("q", (2, T)), ("k", (2, T)), ("v", (2, TB, P)), ("z", (2, 384)), ("az", (2, 384)),
                               ("ez", (2, 384)), ("lz", (2, 384)), ("sp", (2, 512)), ("t", (2, 384)),
                               ("a", (2, 384)), ("oT", (KD, T))):
                r[name], at = region(at, *dims)
            return r

        def places(at, *wanted):
            r = {}
            for name, dims in wanted:
                r[name], at = region(at, *dims)
            assert at <= KEYS * T
            return r

        def attention_regions(a):
            own = ([("mp", (TB, MLA_IN)), ("cn", (TB, QL + KVL)), ("cT", (3, T)), ("q", (TB, HEADS * QD)),
                    ("k", (TB, HEADS * QD)), ("v", (TB, HEADS * 64)), ("qkT", (2, 2, 512))] if a == 0 else
                   [("kv", (TB, 256)), ("kd", (TB, 2, P)), ("kT", (2, T)), ("q", (TB, D)), ("qT", (2, T)),
                    ("nsink", (HEADS,)), ("es", (2, 4))])
            return places(ARENA, *own, ("st", (2, 2, 384)), ("p", (2, 2, 384)), ("pT", (2, 384)), ("nm", (2, 4)),
                          ("su", (2, 4)), ("rc", (4,)), ("oT", (KD, T)), ("rot", (4, HEADS * 16)))

        def ssm_regions():
            r = places(ARENA, ("zs", (TB, DI)), ("xc", (CONV_TILES, T)), ("xs", (TB, DI)), ("X", (TB, DI)),
                       ("Bl", (SG, P)), ("ta", (2, HPG, P)), ("seg", (2, HPG, P)), ("L", (2, HPG, P)),
                       ("M", (2, HPG, P)), ("Xd", (2, T)), ("st", (2, T)), ("t", (2, T)), ("acc", (4, T)),
                       ("u", (64,)), ("az", (64,)), ("ez", (64,)), ("lz", (64,)), ("dt", (64,)), ("a", (64,)),
                       ("acs", (64,)), ("de", (64,)), ("dte", (64,)), ("eacs", (64,)), ("eA", (SH,)))
            r["yT"] = r["xc"]
            return r

        LATE = 88

        def peer_regions():
            r = places(LATE * T, ("s", (TB, SUBS, KEYS)), ("s2", (TB, KEYS)), ("sv", (TB, SUBS, TOPK)),
                       ("si", (TB, SUBS, TOPK)), ("sif", (TB, SUBS, TOPK)), ("cand", (TB, 256)),
                       ("cand2", (TB, 256)), ("bs", (TB, PH, TOPK)), ("bp", (TB * PH * TOPK,)),
                       ("pa", (2, TB * PH * TOPK)), ("pf", (2, TB, PH, TOPK)), ("e", (TB, PH, TOPK)),
                       ("sum", (TB * PH,)), ("rc", (TB * PH,)))
            r["pk"] = split(row[:, :, :].rearrange("p a b -> p (a b)")[:, 0:3 * TB * P], 3, TB, P)
            r["eq"] = split(r["s"][:, 0].rearrange("p m k -> p (m k)"), PH, TOPK, TOPK)
            r["A"] = arena[:, :].rearrange("p (i t) -> p i t", t=T)
            flat = hT[:, :, :].rearrange("p a b -> p (a b)")
            r["hot"] = flat.rearrange("p (s c t k) -> p s c t k", s=2, c=2, t=4)
            r["w"] = flat[:, 0:2 * T].rearrange("p (s t) -> p s t", s=2)
            r["qT"] = pick[:, 0:2, :]
            return r

        block = ctx.enter_context(nc.Block())

        def wait_loaded(e, b, i=None, per_turn=0):
            v = 16 * (b // RING + 1)
            e.wait_ge(loaded[b % RING], v if i is None else i * (16 * per_turn // RING) + v)

        def bank(k, n=1):
            return ps[:, k:k + n, :].rearrange("p a b -> p (a b)")

        def link_for(engine, chain):
            n = [0]

            def link(ins):
                n[0] += 1
                ins.then_inc(chain, 1)
                engine.wait_ge(chain, n[0])
            return link

        x_of = {}
        for n, name in enumerate(LAYERS):
            x_of[name] = n
        x_of["kv"] = x_of["swa"]

        @block.sync
        def _(sp):
            sp.dma_start(x[:, :, :], x_in.rearrange("(b p) d -> p b d", p=P)).then_inc(x_loaded, 16)
            sp.dma_start(cols[:, :], cols_in).then_inc(cols_loaded, 16)
            sp.dma_start(pos[:, :], pos_in).then_inc(pos_loaded, 16)
            for j in range(RING):
                sp.dma_start(ring[:, j, :], stream[j]).then_inc(loaded[j], 16)
            turns = n_blocks // RING - 1
            with sp.Fori(0, turns) as i:
                for j in range(RING):
                    sp.wait_ge(used, i * RING + (j + 1))
                    sp.dma_start(ring[:, j, :], stream[bass.ds(i * RING + (RING + j), 1)]
                                 .rearrange("a p n -> (a p) n")).then_inc(loaded[j], 16)
            for b in range((turns + 1) * RING, n_blocks):
                sp.wait_ge(used, b - RING + 1)
                sp.dma_start(ring[:, b % RING, :], stream[b]).then_inc(loaded[b % RING], 16)
            for b in range(TB):
                sp.wait_ge(of("result"), b + 1)
                sp.dma_start(out[b * P:(b + 1) * P, :], arena[:, b * D:(b + 1) * D]).then_inc(out_done, 16)
            sp.wait_ge(out_done, 16 * TB)

        @block.tensor
        def _(pe):
            ident = col("ident")
            pe.wait_ge(cols_loaded, 16)

            def transposes_of_x(v):
                for k in range(KD):
                    if k < 1:
                        pe.wait_ge(xn_ready, TB * (v + 1 - (v >= NORM_OF["swa"])))
                    for b in range(TB):
                        last = pe.transpose(ps[:, k // 2, (k % 2) * T + b * P:(k % 2) * T + (b + 1) * P],
                                            xn[:, b, k * P:(k + 1) * P], ident)
                    if k % 2:
                        last.then_inc(xT_ready, 1)
                pe.wait_ge(hT_a, 4 * (v + 1))
                pe.wait_ge(hT_d, 4 * (v + 1))

            def by_row_blocks(first, n, lhsT, banks=0):
                for k in range(n):
                    wait_loaded(pe, first + k)
                    for b in range(TB):
                        for half in range(2):
                            last = pe.matmul(ps[:, banks + 2 * b + half, :], lhsT(k, b),
                                             ring[:, (first + k) % RING, half * 512:half * 512 + 512],
                                             start=k == 0, stop=k == n - 1)
                    last.then_inc(used, 1)

            def h_tile(k, b):
                return hT[:, k, b * P:(b + 1) * P]

            def by_column_block(b, dst, i=None, per_turn=0, start=True):
                wait_loaded(pe, b, i, per_turn)
                for k in range(KD):
                    last = pe.matmul(dst, ring[:, b % RING, k * P:(k + 1) * P], hT[:, k, :],
                                     start=k == 0 and start, stop=k == KD - 1)
                last.then_inc(used, 1)

            def ffn(f, name):
                transposes_of_x(NORM_OF[name])
                base, done = AT[name], FC * f
                hid = region(ARENA, 2, 2, T)[0]

                def up(c, b, i=None):
                    by_column_block(b, ps[:, 4 + c % 2, 0:T], i, 12)
                    by_column_block(b + 1, ps[:, 4 + c % 2, T:2 * T], i, 12)

                def down(c, b, i=None, start=False, stop=False):
                    wait_loaded(pe, b, i, 12)
                    for tb in range(TB):
                        for half in range(2):
                            last = pe.matmul(ps[:, 2 * tb + half, :], hid[:, 1, c % 2, tb * P:(tb + 1) * P],
                                             ring[:, b % RING, half * 512:half * 512 + 512],
                                             start=start, stop=stop)
                    last.then_inc(used, 1)

                up(0, base)
                up(1, base + 2)
                pe.wait_ge(hidden_ready, done + 1)
                down(0, base + 4, start=True)
                with pe.Fori(0, 5) as i:
                    for j in range(4):
                        c = 1 + j
                        pe.wait_ge(hidden_ready, i * 4 + (done + c))
                        up(c + 1, base + 2 + 3 * c, i)
                        pe.wait_ge(hidden_ready, i * 4 + (done + c + 1))
                        down(c, base + 4 + 3 * c, i)
                pe.wait_ge(hidden_ready, done + FC)
                down(1, base + 3 * FC - 1, stop=True)

            def stick_breaking():
                transposes_of_x(NORM_OF["sb"])
                base = AT["sb_qkv"]
                R = sb_regions()
                pairs = HEADS // 2

                def project(j, part):
                    b = base + 3 * j
                    if part == 0:
                        if j >= 2:
                            pe.wait_ge(of("sb_qk"), j - 1)
                        by_column_block(b, ps[:, j % 2, 0:T])
                        by_column_block(b + 1, ps[:, j % 2, T:2 * T])
                        return
                    if j >= 2:
                        pe.wait_ge(of("sb_v"), j - 1)
                    wait_loaded(pe, b + 2)
                    for tb in range(TB):
                        for k in range(KD):
                            last = pe.matmul(ps[:, 2 + j % 2, tb * P:(tb + 1) * P], h_tile(k, tb),
                                             ring[:, (b + 2) % RING, k * P:(k + 1) * P],
                                             start=k == 0, stop=k == KD - 1)
                    last.then_inc(used, 1)

                project(0, 0)
                project(0, 1)
                for j in range(pairs):
                    q, k_, v_ = R["q"][:, j % 2], R["k"][:, j % 2], R["v"][:, j % 2]
                    pe.wait_ge(of("sb_qk"), j + 1)
                    if j >= 1:
                        pe.wait_ge(of("sb_o"), j)
                    for e in range(2):
                        h = slice(64 * e, 64 * e + 64)
                        pe.matmul(ps[:, 4 + e, 0:T], k_[h, 0:P], q[h, :], start=True, stop=True)
                        last = pe.matmul(ps[:, 4 + e, T:T + P], k_[h, P:T], q[h, P:T], start=True, stop=True)
                    last.then_inc(of("sb_s"), 1)
                    if j + 1 < pairs:
                        project(j + 1, 0)
                    pe.wait_ge(of("sb_sp"), j + 1)
                    if j >= 1:
                        pe.wait_ge(of("sb_t"), j)
                    for e in range(2):
                        sp_ = R["sp"][:, e]
                        pe.matmul(ps[:, 6 + e, 0:T], col("lo_incl"), sp_[:, 0:T], start=True, stop=False)
                        pe.matmul(ps[:, 6 + e, P:T], col("ones"), sp_[:, T:T + P], start=False, stop=True)
                        last = pe.matmul(ps[:, 6 + e, T:T + P], col("lo_incl"), sp_[:, T:T + P],
                                         start=True, stop=True)
                    last.then_inc(of("sb_r"), 1)
                    if j + 1 < pairs:
                        project(j + 1, 1)
                    pe.wait_ge(of("sb_a"), j + 1)
                    pe.wait_ge(of("sb_v"), j + 1)
                    for e in range(2):
                        o = ps[64 * e:64 * e + 64, 4, 0:T]
                        a_ = R["a"][:, e]
                        pe.matmul(o, v_[:, 0, 64 * e:64 * e + 64], a_[:, 0:T], start=True, stop=False)
                        last = pe.matmul(ps[64 * e:64 * e + 64, 4, P:T], v_[:, 1, 64 * e:64 * e + 64],
                                         a_[:, T:T + P], start=False, stop=True)
                    last.then_inc(of("sb_av"), 1)
                pe.wait_ge(of("sb_o"), pairs)
                by_row_blocks(AT["sb_out"], KD, lambda k, b: R["oT"][:, k, b * P:(b + 1) * P])

            def attention(a, R, scores_ready):
                pairs, n0 = HEADS // 2, a * (HEADS // 2)

                def turn_q(j):
                    if j >= 1:
                        pe.wait_ge(of("att_qk"), n0 + j)
                    if a == 0:
                        for e in range(2):
                            for part in range(2):
                                src = R["qk"[part]]
                                for tb in range(TB):
                                    h = (2 * j + e) * QD
                                    o = part * T + tb * P
                                    last = pe.transpose(ps[0:QD, e, o:o + P], src[:, tb, h:h + QD], ident)
                    else:
                        for tb in range(TB):
                            last = pe.transpose(ps[:, 0, tb * P:(tb + 1) * P],
                                                R["q"][:, tb, j * P:(j + 1) * P], ident)
                    last.then_inc(of("att_t"), 1)

                def scores(j):
                    pe.wait_ge(of("att_qk"), n0 + j + 1)
                    if j >= 1:
                        pe.wait_ge(of("att_m"), n0 + j)
                    for e in range(2):
                        if a == 0:
                            qT, kT = R["qkT"][0:QD, j % 2, e, 0:T], R["qkT"][0:QD, j % 2, e, T:2 * T]
                        else:
                            h = slice(64 * e, 64 * e + 64)
                            qT, kT = R["qT"][h, j % 2, :], R["kT"][h, 2 * j // 8, :]
                        pe.matmul(ps[:, 2 + e, 0:P], qT[:, 0:P], kT[:, 0:P], start=True, stop=True)
                        last = pe.matmul(ps[:, 2 + e, P:3 * P], qT[:, P:T], kT, start=True, stop=True)
                    last.then_inc(of("att_s"), 1)

                def turn_p(j):
                    pe.wait_ge(of("att_n"), n0 + j + 1)
                    if j >= 1:
                        pe.wait_ge(of("att_w"), n0 + j)
                    for e in range(2):
                        for s in range(3):
                            last = pe.transpose(ps[:, 4 + e, s * P:(s + 1) * P],
                                                R["p"][:, j % 2, e, s * P:(s + 1) * P], ident)
                    last.then_inc(of("att_pT"), 1)

                def values(j):
                    pe.wait_ge(of("att_w"), n0 + j + 1)
                    if j >= 2:
                        pe.wait_ge(of("att_o"), n0 + j - 1)
                    for e in range(2):
                        h = slice(64 * e, 64 * e + 64)
                        for kb in range(TB):
                            if a == 0:
                                v = R["v"][:, kb, (2 * j + e) * 64:(2 * j + e) * 64 + 64]
                            else:
                                o = P + (2 * j // 8) * 64
                                v = R["kv"][:, kb, o:o + 64]
                            last = pe.matmul(ps[h, 6 + j % 2, kb * P:T], v, R["pT"][:, e, kb * T:T + kb * P],
                                             start=kb == 0, stop=kb == 1)
                    last.then_inc(of("att_av"), 1)

                turn_q(0)
                scores(0)
                turn_q(1)
                for j in range(pairs):
                    if j + 1 < pairs:
                        scores(j + 1)
                    turn_p(j)
                    if j + 2 < pairs:
                        turn_q(j + 2)
                    values(j)
                pe.wait_ge(of("att_o"), n0 + pairs)
                by_row_blocks(AT["mla_out"] if a == 0 else AT["swa_out"], KD,
                              lambda k, b: R["oT"][:, k, b * P:(b + 1) * P])

            def mla():
                transposes_of_x(NORM_OF["mla"])
                R = attention_regions(0)
                base = AT["mla_in"]
                for k in range(KD):
                    b = base + k // 2
                    if k % 2 == 0:
                        wait_loaded(pe, b)
                    for tb in range(TB):
                        last = pe.matmul(ps[:, tb, 0:MLA_IN], h_tile(k, tb),
                                         ring[:, b % RING, (k % 2) * MLA_IN:(k % 2 + 1) * MLA_IN],
                                         start=k == 0, stop=k == KD - 1)
                    if k % 2:
                        last.then_inc(used, 1)
                pe.wait_ge(of("mla_cn"), 1)
                for c in range(3):
                    for tb in range(TB):
                        last = pe.transpose(ps[:, 2 + c // 2, (c % 2) * T + tb * P:(c % 2) * T + (tb + 1) * P],
                                            R["cn"][:, tb, c * P:(c + 1) * P], ident)
                last.then_inc(of("mla_cT"), 1)
                pe.wait_ge(of("mla_cTs"), 1)
                for n in range(3):
                    b = AT["mla_uq"] + n
                    wait_loaded(pe, b)
                    for tb in range(TB):
                        for k in range(2):
                            last = pe.matmul(ps[:, 4 * tb + n, :], R["cT"][:, k, tb * P:(tb + 1) * P],
                                             ring[:, b % RING, k * 512:(k + 1) * 512], start=k == 0, stop=k == 1)
                    last.then_inc(used, 1)
                pe.wait_ge(of("mla_q"), 1)
                for n in range(2):
                    b = AT["mla_ukv"] + n
                    wait_loaded(pe, b)
                    for tb in range(TB):
                        for half in range(2):
                            last = pe.matmul(ps[:, 4 * tb + 2 * n + half, :], R["cT"][:, 2, tb * P:(tb + 1) * P],
                                             ring[:, b % RING, half * 512:(half + 1) * 512], start=True, stop=True)
                    last.then_inc(used, 1)
                pe.wait_ge(of("mla_kv_a"), 1)
                pe.wait_ge(of("mla_kv_d"), 1)
                attention(0, R, None)

            def swa():
                R = attention_regions(1)
                transposes_of_x(NORM_OF["kv"])
                for k in range(KD):
                    b = AT["swa_kv"] + k // 4
                    if k % 4 == 0:
                        wait_loaded(pe, b)
                    for tb in range(TB):
                        last = pe.matmul(ps[:, 4 + tb, 0:256], h_tile(k, tb),
                                         ring[:, b % RING, (k % 4) * 256:(k % 4 + 1) * 256],
                                         start=k == 0, stop=k == KD - 1)
                    if k % 4 == 3:
                        last.then_inc(used, 1)
                transposes_of_x(NORM_OF["swa"])
                by_row_blocks(AT["swa_q"], KD, h_tile)
                pe.wait_ge(of("swa_k"), 1)
                for g in range(2):
                    for tb in range(TB):
                        last = pe.transpose(ps[:, 6, g * T + tb * P:g * T + (tb + 1) * P], R["kd"][:, tb, g, :], ident)
                last.then_inc(of("swa_kT"), 1)
                pe.wait_ge(of("swa_q"), 1)
                pe.wait_ge(of("swa_kTs"), 1)
                attention(1, R, None)

            def ssm():
                R = ssm_regions()
                transposes_of_x(NORM_OF["ssm"])
                for half in range(2):
                    by_row_blocks(AT["ssm_z"] + 8 * half, KD, h_tile, banks=4 * half)
                base = AT["ssm_xbc"]
                pe.wait_ge(of("ssm_z"), 1)
                for c in range(4):
                    by_column_block(base + c, ps[:, c, 0:T])
                with pe.Fori(0, CONV_TILES // 4 - 1) as i:
                    for j in range(4):
                        pe.wait_ge(of("conv_taps"), i * 12 + (3 * j + 3))
                        by_column_block(base + 4 + j, ps[:, j, 0:T], i, 4)
                pe.wait_ge(of("ssm_z"), 2)
                b = AT["ssm_dt"]
                wait_loaded(pe, b)
                for tb in range(TB):
                    for k in range(KD):
                        last = pe.matmul(ps[:, 4, tb * SH:(tb + 1) * SH], h_tile(k, tb),
                                         ring[:, b % RING, k * SH:(k + 1) * SH], start=k == 0, stop=k == KD - 1)
                last.then_inc(used, 1)
                pe.wait_ge(of("ssm_a"), 1)
                pe.matmul(ps[:, 5, 0:64], col("up_incl"), R["a"], start=True, stop=True)
                pe.matmul(ps[:, 5, 64:128], col("ones"), R["a"], start=True, stop=True).then_inc(of("ssm_cs"), 1)
                pe.wait_ge(of("conv_done"), CONV_TILES)
                for n in range(8):
                    if n >= 4:
                        pe.wait_ge(of("ssm_xs"), n - 3)
                    for q in range(4):
                        last = pe.transpose(ps[:, n % 4, q * P:(q + 1) * P],
                                            R["xc"][:, 4 * (n // 2) + q, (n % 2) * P:(n % 2 + 1) * P], ident)
                    last.then_inc(of("ssm_xT"), 1)
                for n in range(2):
                    for q in range(4):
                        last = pe.transpose(ps[:, 6 + n, q * P:(q + 1) * P], R["xc"][:, 16 + 4 * n + q, 0:P], ident)
                    last.then_inc(of("ssm_xT"), 1)
                pe.wait_ge(of("ssm_xs"), 10)

                def sums(n):
                    g, c = n // 2, n % 2
                    pe.wait_ge(of("sg_ta"), n + 1)
                    if n >= 2:
                        pe.wait_ge(of("sg_seg"), n - 1)
                        pe.wait_ge(of("sg_M"), n - 1)
                    pe.matmul(ps[:, n % 2, :], col("ones"), R["ta"][:, n % 2].rearrange("p a b -> p (a b)"),
                              start=True, stop=True)
                    pe.matmul(ps[:, 2 + n % 2, 0:P], R["xc"][:, 16 + g, c * P:(c + 1) * P],
                              R["xc"][:, 24 + g, c * P:(c + 1) * P], start=True, stop=True).then_inc(of("sg_cb"), 1)

                sums(0)
                for n in range(2 * SG):
                    g, c = n // 2, n % 2
                    if n + 1 < 2 * SG:
                        sums(n + 1)
                    pe.wait_ge(of("sg_M"), n + 1)
                    if n >= 2:
                        pe.wait_ge(of("sg_o"), n - 1)
                    if c == 0 and g >= 2:
                        pe.wait_ge(of("sg_st"), g - 1)
                    if c == 1:
                        pe.wait_ge(of("sg_st"), g + 1)
                    for q in range(HPG):
                        o = (HPG * g + q) * 64
                        last = pe.matmul(ps[:, 4 + n % 2, q * 64:(q + 1) * 64], R["M"][:, n % 2, q, :],
                                         R["X"][:, c, o:o + 64], start=True, stop=True)
                    if c == 0:
                        last = pe.matmul(ps[:, 6 + g % 2, 0:T], R["Bl"][:, g, :], R["Xd"][:, g % 2, :],
                                         start=True, stop=True)
                    else:
                        last = pe.matmul(ps[:, 4 + n % 2, T:2 * T], R["xc"][:, 24 + g, P:T], R["st"][:, g % 2, :],
                                         start=True, stop=True)
                    last.then_inc(of("sg_y"), 1)
                pe.wait_ge(of("ssm_yn"), TB)
                for k in range(DI // P):
                    for tb in range(TB):
                        last = pe.transpose(ps[:, k // 2, (k % 2) * T + tb * P:(k % 2) * T + (tb + 1) * P],
                                            R["zs"][:, tb, k * P:(k + 1) * P], ident)
                    if k % 2:
                        last.then_inc(of("ssm_yT"), 1)
                pe.wait_ge(of("ssm_yT_a"), 8)
                pe.wait_ge(of("ssm_yT_d"), 8)
                by_row_blocks(AT["ssm_out"], DI // P, lambda k, b: R["yT"][:, k, b * P:(b + 1) * P])

            def peer(l):
                R = peer_regions()
                transposes_of_x(NORM_OF[f"peer{l}"])
                base, n0 = AT[f"peer{l}_q"], SUBS * l
                subkeys = col("subkeys", 2, 2, KEYS)

                def key_scores(m):
                    pe.wait_ge(of("peer_qT"), n0 + m + 1)
                    if m >= 2:
                        pe.wait_ge(of("peer_s"), n0 + m - 1)
                    for tb in range(TB):
                        last = pe.matmul(ps[:, 2 + m % 2, tb * P:(tb + 1) * P],
                                         R["qT"][:, m % 2, tb * P:(tb + 1) * P], subkeys[:, l, m % 2, :],
                                         start=True, stop=True)
                    last.then_inc(of("peer_sp"), 1)

                for m in range(SUBS):
                    if m >= 2:
                        pe.wait_ge(of("peer_qT"), n0 + m - 1)
                    by_column_block(base + m, ps[:, m % 2, 0:T])
                    if m >= 1:
                        key_scores(m - 1)
                key_scores(SUBS - 1)
                base, n0 = AT[f"peer{l}_u"], 64 * l
                for n in range(4):
                    for j in range(2):
                        by_column_block(base + 2 * n + j, ps[:, 4 + n, j * T:(j + 1) * T])
                with pe.Fori(0, KEYS // 8 - 1) as i:
                    for n in range(4):
                        pe.wait_ge(of("gelu"), i * 4 + (n0 + n + 1))
                        for j in range(2):
                            by_column_block(base + 8 + 2 * n + j, ps[:, 4 + n, j * T:(j + 1) * T], i, 8)
                pe.wait_ge(of("picks"), l + 1)
                for c in range(3):
                    for tb in range(TB):
                        last = pe.transpose(ps[:, c // 2, (c % 2) * T + tb * P:(c % 2) * T + (tb + 1) * P],
                                            R["pk"][:, c, tb, :], ident)
                last.then_inc(of("picksT"), 1)
                pe.wait_ge(of("picksTs"), l + 1)

                def gates(n):
                    for q in range(4):
                        last = pe.matmul(ps[:, n, q * P:(q + 1) * P], R["hot"][:, n % 2, 0, q, :],
                                         R["hot"][:, n % 2, 1, q, :], start=True, stop=True)
                    last.then_inc(of("gates"), 1)

                for n in range(4):
                    pe.wait_ge(of("hot"), n0 + n + 1)
                    gates(n)
                with pe.Fori(0, 15) as i:
                    for n in range(4):
                        pe.wait_ge(of("hot"), i * 4 + (n0 + n + 5))
                        pe.wait_ge(of("gated"), i * 4 + (n0 + n + 1))
                        gates(n)
                pe.wait_ge(of("gated"), n0 + 64)
                base, n0 = AT[f"peer{l}_v"], KEYS * l

                def down(j, i=None, start=False, stop=False):
                    wait_loaded(pe, base + j, i, 4)
                    pe.wait_ge(of("peer_w"), n0 + j + 1 if i is None else i * 4 + (n0 + j + 1))
                    for tb in range(TB):
                        for half in range(2):
                            last = pe.matmul(ps[:, 2 * tb + half, :], R["w"][:, j % 2, tb * P:(tb + 1) * P],
                                             ring[:, (base + j) % RING, half * 512:(half + 1) * 512],
                                             start=start, stop=stop)
                    last.then_inc(used, 1)

                for j in range(4):
                    down(j, start=j == 0)
                with pe.Fori(0, KEYS // 4 - 2) as i:
                    for j in range(4, 8):
                        down(j, i)
                for j in range(KEYS - 4, KEYS):
                    down(j, stop=j == KEYS - 1)

            def ple(l):
                transposes_of_x(NORM_OF[f"ple{l}"])
                by_row_blocks(AT[f"ple{l}_gate"], KD, h_tile)
                pT = col("pT", 2, 2, T)
                by_row_blocks(AT[f"ple{l}_proj"], 2, lambda k, b: pT[:, l, k, b * P:(b + 1) * P], banks=4)


            fs = 0
            for name in layers:
                if name.startswith("ffn"):
                    ffn(fs, name)
                    fs += 1
                elif name == "sb":
                    stick_breaking()
                elif name in ("mla", "swa", "ssm"):
                    {"mla": mla, "swa": swa, "ssm": ssm}[name]()
                elif name.startswith("peer"):
                    peer(int(name[-1]))
                elif name.startswith("ple"):
                    ple(int(name[-1]))

        @block.scalar
        def _(act):
            link = link_for(act, act_chain)
            rows_used = [0, 0]

            def load_row(n, slot):
                act.dma_start(row[:, slot, :], rows_in[n:n + 1, :].rearrange("a n -> (a n)")
                              .partition_broadcast(P)).then_inc(row_loaded[slot], 16)

            def squares(parts, into=arena):
                at = 0
                for n, (src, w) in enumerate(parts):
                    junk = into[:, at:at + w]
                    at += w
                    last = act.activation(junk, src, ACT.Square, accum_out=ss[:, n:n + 1])
                last.then_inc(ss_ready, 1)

            def norm_in(name):
                v = NORM_OF[name]
                if name != "swa":
                    act.wait_ge(x_ready, x_of[name]) if x_of[name] else act.wait_ge(x_loaded, 16)
                    squares([(x[:, b, :], D) for b in range(TB)])
                for k in (0, 1, 4, 5):
                    act.wait_ge(xT_ready, 4 * v + k // 2 + 1)
                    act.activation(hT[:, k, :], ps[:, k // 2, (k % 2) * T:(k % 2 + 1) * T], ACT.Copy,
                                   scale=gain(v, k)).then_inc(hT_a, 1)

            def squares_of_banks():
                squares([(bank(2 * b, 2), D) for b in range(TB)])

            def ffn(f, name):
                norm_in(name)
                load_row(f if f == 0 else {1: 2, 2: 3, 3: 5}[f], 0)
                base, done = AT[name], FC * f
                hid = region(ARENA, 2, 2, T)[0]

                def silu(c):
                    return act.activation(hid[:, 0, c % 2, :], ps[:, 4 + c % 2, 0:T], ACT.Silu)

                act.wait_ge(used, base + 2)
                silu(0).then_inc(silu_ready, 1)
                act.wait_ge(used, base + 4)
                silu(1).then_inc(silu_ready, 1)
                with act.Fori(0, 5) as i:
                    for j in range(4):
                        c = 2 + j
                        act.wait_ge(used, i * 12 + (base + 3 * c + 1))
                        act.wait_ge(hidden_ready, i * 4 + (done + c - 1))
                        silu(c).then_inc(silu_ready, 1)
                act.wait_ge(used, base + 3 * FC)
                squares_of_banks()

            def stick_breaking():
                norm_in("sb")
                load_row(1, 0)
                base = AT["sb_qkv"]
                R = sb_regions()
                pairs = HEADS // 2

                def evac(j):
                    if j >= 2:
                        act.wait_ge(of("sb_av"), j - 1)
                    act.wait_ge(used, base + 3 * j + 2)
                    act.activation(R["q"][:, j % 2], ps[:, j % 2, 0:T], ACT.Copy, scale=0.125)
                    act.activation(R["k"][:, j % 2], ps[:, j % 2, T:2 * T], ACT.Copy).then_inc(of("sb_qk"), 1)

                evac(0)
                for j in range(pairs):
                    act.wait_ge(of("sb_s"), j + 1)
                    act.wait_ge(of("sb_sp"), j) if j else None
                    link(act.activation(R["az"][:, :, :], ps[:, 4:6, 0:384], ACT.Abs))
                    link(act.activation(R["ez"][:, :, :], R["az"][:, :, :], ACT.Exp, scale=-1.0))
                    act.activation(R["lz"][:, :, :], R["ez"][:, :, :], ACT.Ln, bias=1.0).then_inc(of("sb_l"), 1)
                    if j + 1 < pairs:
                        evac(j + 1)
                    act.wait_ge(of("sb_t"), j + 1)
                    act.wait_ge(of("sb_av"), j) if j else None
                    act.activation(R["a"][:, :, :], R["t"][:, :, :], ACT.Exp).then_inc(of("sb_a"), 1)
                act.wait_ge(used, AT["sb_out"] + KD)
                squares_of_banks()

            def attention(a, R):
                pairs, n0 = HEADS // 2, a * (HEADS // 2)

                def take_q(j):
                    act.wait_ge(of("att_t"), n0 + j + 1)
                    if j >= 2:
                        act.wait_ge(of("att_s"), n0 + j - 1)
                    if a == 0:
                        act.activation(R["qkT"][0:QD, j % 2], ps[0:QD, 0:2, :], ACT.Copy).then_inc(of("att_qk"), 1)
                    else:
                        act.activation(R["qT"][:, j % 2], ps[:, 0, 0:T], ACT.Copy).then_inc(of("att_qk"), 1)

                def exps(j):
                    act.wait_ge(of("att_m"), n0 + j + 1)
                    if j >= 2:
                        act.wait_ge(of("att_pT"), n0 + j - 1)
                    for e in range(2):
                        for tb in range(TB):
                            c = slice(0, P) if tb == 0 else slice(P, 3 * P)
                            k = 2 * e + tb
                            last = act.activation(R["p"][:, j % 2, e, c], R["st"][:, j % 2, e, c], ACT.Exp,
                                                  bias=R["nm"][:, j % 2, k:k + 1],
                                                  accum_out=R["su"][:, j % 2, k:k + 1])
                        if a:
                            last = act.activation(R["es"][:, j % 2, 2 * e:2 * e + 2],
                                                  R["nm"][:, j % 2, 2 * e:2 * e + 2], ACT.Exp,
                                                  bias=col("sinks")[:, 2 * j + e:2 * j + e + 1])
                    last.then_inc(of("att_p"), 1)

                def take_p(j):
                    act.wait_ge(of("att_pT"), n0 + j + 1)
                    if j >= 1:
                        act.wait_ge(of("att_av"), n0 + j)
                    act.activation(R["pT"][:, :, :], ps[:, 4:6, 0:384], ACT.Copy).then_inc(of("att_w"), 1)

                take_q(0)
                take_q(1)
                exps(0)
                for j in range(pairs):
                    if j + 1 < pairs:
                        exps(j + 1)
                    take_p(j)
                    if j + 2 < pairs:
                        take_q(j + 2)

            def mla():
                norm_in("mla")
                load_row(4, 0)
                R = attention_regions(0)
                act.wait_ge(used, AT["mla_in"] + 4)
                for tb in range(TB):
                    last = act.activation(R["mp"][:, tb, :], ps[:, tb, 0:MLA_IN], ACT.Copy)
                link(last)
                squares([(R["mp"][:, tb, 0:QL], QL) for tb in range(TB)] +
                        [(R["mp"][:, tb, QL:QL + KVL], KVL) for tb in range(TB)])
                act.wait_ge(of("mla_cT"), 1)
                for c in range(3):
                    g = col("q_norm")[:, c:c + 1] if c < 2 else col("kv_norm")
                    last = act.activation(R["cT"][:, c, :], ps[:, 2 + c // 2, (c % 2) * T:(c % 2 + 1) * T],
                                          ACT.Copy, scale=g)
                last.then_inc(of("mla_cTs"), 1)
                act.wait_ge(used, AT["mla_uq"] + 3)
                for tb in range(TB):
                    last = act.activation(R["q"][:, tb, :], bank(4 * tb, 3), ACT.Copy)
                last.then_inc(of("mla_q"), 1)
                act.wait_ge(used, AT["mla_ukv"] + 2)
                kv = bank(0, 4).rearrange("p (h c) -> p h c", h=HEADS)
                act.activation(split(R["k"][:, 0, :], HEADS, QD)[:, :, 0:64], kv[:, :, 0:64], ACT.Copy)
                act.activation(split(R["v"][:, 0, :], HEADS, 64), kv[:, :, 64:128], ACT.Copy)\
                   .then_inc(of("mla_kv_a"), 1)
                attention(0, R)
                act.wait_ge(used, AT["mla_out"] + KD)
                squares_of_banks()

            def swa():
                R = attention_regions(1)
                norm_in("kv")
                load_row(6, 0)
                load_row(8, 1)
                norm_in("swa")
                act.wait_ge(of("swa_kT"), 1)
                act.activation(R["kT"][:, :, :], ps[:, 6, :].rearrange("p (g t) -> p g t", g=2), ACT.Copy)\
                   .then_inc(of("swa_kTs"), 1)
                attention(1, R)

            def ssm():
                R = ssm_regions()
                norm_in("ssm")
                for half in range(2):
                    act.wait_ge(used, AT["ssm_z"] + 8 * half + 8)
                    for b in range(TB):
                        last = act.activation(R["zs"][:, b, half * D:(half + 1) * D], bank(4 * half + 2 * b, 2),
                                              ACT.Silu)
                    last.then_inc(of("ssm_z"), 1)
                base = AT["ssm_xbc"]
                conv = CAT["conv"][0]
                with act.Fori(0, CONV_TILES // 4) as i:
                    for j in range(4):
                        act.wait_ge(used, i * 4 + (base + j + 1))
                        o = i * 20 + (conv + 5 * j)
                        act.activation(R["acc"][:, j, :], ps[:, j, 0:T], ACT.Identity,
                                       scale=cols[:, bass.ds(o + 3, 1)], bias=cols[:, bass.ds(o + 4, 1)])\
                           .then_inc(of("conv_acc"), 1)
                        act.wait_ge(of("conv_taps"), i * 12 + (3 * j + 3))
                        act.activation(R["xc"][:, bass.ds(i * 4 + j, 1), :].rearrange("p a t -> p (a t)"),
                                       R["acc"][:, j, :], ACT.Silu).then_inc(of("conv_done"), 1)
                act.wait_ge(of("ssm_u"), 1)
                act.activation(R["eA"], col("a_log"), ACT.Exp)
                link(act.activation(R["az"], R["u"], ACT.Abs))
                link(act.activation(R["ez"], R["az"], ACT.Exp, scale=-1.0))
                act.activation(R["lz"], R["ez"], ACT.Ln, bias=1.0).then_inc(of("ssm_l"), 1)
                act.wait_ge(of("ssm_de"), 1)
                act.activation(R["dte"], R["de"], ACT.Exp)
                act.activation(R["eacs"], R["acs"], ACT.Exp).then_inc(of("ssm_ex"), 1)
                for n in range(8):
                    act.wait_ge(of("ssm_xT"), n + 1)
                    act.activation(R["xs"][:, n % 2, (n // 2) * 512:(n // 2 + 1) * 512], ps[:, n % 4, :], ACT.Copy)\
                       .then_inc(of("ssm_xs"), 1)
                for n in range(2):
                    act.wait_ge(of("ssm_xT"), 9 + n)
                    act.activation(R["Bl"][:, 4 * n:4 * n + 4, :].rearrange("p a b -> p (a b)"), ps[:, 6 + n, :],
                                   ACT.Copy).then_inc(of("ssm_xs"), 1)

                def state(g):
                    act.wait_ge(of("sg_y"), 2 * g + 1)
                    act.activation(R["st"][:, g % 2, :], ps[:, 6 + g % 2, 0:T], ACT.Copy).then_inc(of("sg_st"), 1)

                for n in range(2 * SG):
                    act.wait_ge(of("sg_seg"), n + 1)
                    if n >= 2:
                        act.wait_ge(of("sg_M"), n - 1)
                    act.activation(R["L"][:, n % 2], R["seg"][:, n % 2], ACT.Exp).then_inc(of("sg_L"), 1)
                    if n % 2:
                        state(n // 2)
                act.wait_ge(of("sg_done"), 2 * SG)
                squares([(R["zs"][:, tb, g * T:(g + 1) * T], T) for tb in range(TB) for g in range(SG)],
                        R["X"][:, :, :].rearrange("p a b -> p (a b)"))
                for k in (0, 1, 4, 5, 8, 9, 12, 13):
                    act.wait_ge(of("ssm_yT"), k // 2 + 1)
                    act.activation(R["yT"][:, k, :], ps[:, k // 2, (k % 2) * T:(k % 2 + 1) * T], ACT.Copy,
                                   scale=col("gate_norm")[:, k:k + 1]).then_inc(of("ssm_yT_a"), 1)

            def peer(l):
                R = peer_regions()
                norm_in(f"peer{l}")
                base, n0 = AT[f"peer{l}_q"], SUBS * l
                for m in range(SUBS):
                    act.wait_ge(used, base + m + 1)
                    if m >= 2:
                        act.wait_ge(of("peer_sp"), n0 + m - 1)
                    act.activation(R["qT"][:, m % 2, :], ps[:, m % 2, 0:T], ACT.Copy).then_inc(of("peer_qT"), 1)
                base, n0 = AT[f"peer{l}_u"], 64 * l

                def gelus(first, turns):
                    with act.Fori(0, turns) as i:
                        for n in range(4):
                            act.wait_ge(used, i * 8 + (base + first + 2 * n + 2))
                            act.activation(R["A"][:, bass.ds(i * 8 + (first + 2 * n), 2), :]
                                           .rearrange("p a t -> p (a t)"), ps[:, 4 + n, :], ACT.Gelu)\
                               .then_inc(of("gelu"), 1)

                gelus(0, LATE // 8)
                act.wait_ge(of("peer_e"), l + 1)
                act.activation(R["e"], R["e"], ACT.Exp).then_inc(of("peer_ex"), 1)
                act.wait_ge(of("picks"), l + 1)
                gelus(LATE, (KEYS - LATE) // 8)
                act.wait_ge(of("picksT"), l + 1)
                act.activation(pick[:, 0:2, :], ps[:, 0, :].rearrange("p (a t) -> p a t", a=2), ACT.Copy)
                act.activation(pick[:, 2, :], ps[:, 1, 0:T], ACT.Copy).then_inc(of("picksTs"), 1)
                act.wait_ge(of("gated"), 64 * l + 64)
                base, n0 = AT[f"peer{l}_v"], KEYS * l

                def take(j, i=None):
                    at = j if i is None else i * 4 + j
                    if j >= 2:
                        act.wait_ge(used, at + (base - 1))
                    act.activation(R["w"][:, j % 2, :], R["A"][:, bass.ds(at, 1), :].rearrange("p a t -> p (a t)")
                                   if i is not None else R["A"][:, j, :], ACT.Copy).then_inc(of("peer_w"), 1)

                for j in range(4):
                    take(j)
                with act.Fori(0, KEYS // 4 - 1) as i:
                    for j in range(4, 8):
                        take(j, i)

            def ple(l):
                norm_in(f"ple{l}")
                act.wait_ge(used, AT[f"ple{l}_gate"] + KD)
                sg = region(ARENA, TB, D)[0]
                for b in range(TB):
                    last = act.activation(sg[:, b, :], bank(2 * b, 2), ACT.Sigmoid)
                last.then_inc(of("ple_gate"), 1)


            act.wait_ge(cols_loaded, 16)
            act.wait_ge(of("angle"), 1)
            act.activation(ang[:, 2], ang[:, 1], ACT.Abs).then_inc(of("angle_abs"), 1)
            act.wait_ge(of("angle"), 2)
            act.activation(sinT[:, :, :], ang[:, 1], ACT.Sin)
            act.activation(cosT[:, :, :], ang[:, 3], ACT.Sin).then_inc(of("angle_sin"), 1)
            fs = 0
            for name in layers:
                if name.startswith("ffn"):
                    ffn(fs, name)
                    fs += 1
                elif name == "sb":
                    stick_breaking()
                elif name in ("mla", "swa", "ssm"):
                    {"mla": mla, "swa": swa, "ssm": ssm}[name]()
                elif name.startswith("peer"):
                    peer(int(name[-1]))
                elif name.startswith("ple"):
                    ple(int(name[-1]))
            if stop == len(LAYERS):
                act.wait_ge(x_ready, len(LAYERS))
                load_row(7, 0)
                squares([(x[:, b, :], D) for b in range(TB)])

        @block.vector
        def _(dve):
            link = link_for(dve, dve_chain)
            stats = [0]
            rows = [0, 0]

            def row_wait(slot):
                rows[slot] += 16
                dve.wait_ge(row_loaded[slot], rows[slot])

            def rstd(parts):
                stats[0] += 1
                dve.wait_ge(ss_ready, stats[0])
                for a, b, scale, eps in parts:
                    last = dve.tensor_scalar(ms[:, a:b], ss[:, a:b], scale, eps, ALU.mult, ALU.add)
                last.then_inc(ms_ready, 1)
                dve.wait_ge(rs_ready, stats[0])

            def norm_in(name):
                v = NORM_OF[name]
                if name != "swa":
                    rstd([(0, TB, 1.0 / D, EPS)])
                    for b in range(TB):
                        dve.tensor_scalar(xn[:, b, :], x[:, b, :], rs[:, b:b + 1], None, ALU.mult)\
                           .then_inc(xn_ready, 1)
                for k in (2, 3, 6, 7):
                    dve.wait_ge(xT_ready, 4 * v + k // 2 + 1)
                    dve.tensor_scalar(hT[:, k, :], ps[:, k // 2, (k % 2) * T:(k % 2 + 1) * T], gain(v, k),
                                      None, ALU.mult).then_inc(hT_d, 1)

            def add_normed(weight):
                rstd([(0, TB, 1.0 / (D * weight * weight), EPS / (weight * weight))])
                row_wait(0)
                for b in range(TB):
                    link(dve.scalar_tensor_tensor(xn[:, b, :], bank(2 * b, 2), rs[:, b:b + 1],
                                                  row[:, 0, :], ALU.mult, ALU.mult))
                    last = dve.tensor_tensor(x[:, b, :], x[:, b, :], xn[:, b, :], ALU.add)
                last.then_inc(x_ready, 1)

            def ffn(f, name):
                norm_in(name)
                base, done = AT[name], FC * f
                hid = region(ARENA, 2, 2, T)[0]

                def hidden(c):
                    dve.tensor_tensor(hid[:, 1, c % 2, :], ps[:, 4 + c % 2, T:2 * T], hid[:, 0, c % 2, :],
                                      ALU.mult).then_inc(hidden_ready, 1)

                for c in range(2):
                    dve.wait_ge(silu_ready, done + c + 1)
                    hidden(c)
                with dve.Fori(0, 5) as i:
                    for j in range(4):
                        c = 2 + j
                        dve.wait_ge(silu_ready, i * 4 + (done + c + 1))
                        dve.wait_ge(used, i * 12 + (base + 3 * c - 1))
                        hidden(c)
                add_normed(0.5)

            def stick_breaking():
                norm_in("sb")
                base = AT["sb_qkv"]
                R = sb_regions()
                pairs = HEADS // 2

                def evac(j):
                    if j >= 2:
                        dve.wait_ge(of("sb_av"), j - 1)
                    dve.wait_ge(used, base + 3 * j + 3)
                    dve.tensor_copy(R["v"][:, j % 2], ps[:, 2 + j % 2, 0:T].rearrange("p (a b) -> p a b", a=TB))\
                       .then_inc(of("sb_v"), 1)

                evac(0)
                for j in range(pairs):
                    dve.wait_ge(of("sb_l"), j + 1)
                    dve.tensor_copy(R["z"][:, :, :], ps[:, 4:6, 0:384])
                    dve.wait_ge(of("sb_r"), j) if j else None
                    link(dve.scalar_tensor_tensor(R["sp"][:, :, 0:384], ps[:, 4:6, 0:384], 0.0,
                                                  R["lz"][:, :, :], ALU.max, ALU.add))
                    for e in range(2):
                        diag = R["sp"][:, e].rearrange("p (a b) -> p a b", a=2)[:, :, 0:P]
                        last = dve.tensor_tensor(diag, diag, col("up_strict").unsqueeze(1)
                                                 .to_broadcast([P, 2, P]), ALU.mult)
                    last.then_inc(of("sb_sp"), 1)
                    dve.wait_ge(of("sb_r"), j + 1)
                    dve.wait_ge(of("sb_a"), j) if j else None
                    link(dve.tensor_tensor(R["t"][:, :, :], R["z"][:, :, :], ps[:, 6:8, 0:384], ALU.subtract))
                    for e in range(2):
                        for s in range(2):
                            diag = R["t"][:, e, s * T:s * T + P]
                            last = dve.tensor_tensor(diag, diag, col("neg_strict"), ALU.add)
                    last.then_inc(of("sb_t"), 1)
                    if j + 1 < pairs:
                        evac(j + 1)
                    dve.wait_ge(of("sb_av"), j + 1)
                    dve.tensor_copy(R["oT"][:, j, :], ps[:, 4, 0:T]).then_inc(of("sb_o"), 1)
                add_normed(1.0)

            def add(*sources):
                for b in range(TB):
                    y = bank(2 * b, 2)
                    if sources:
                        link(dve.tensor_tensor(xn[:, b, :], y, sources[0], ALU.add))
                        y = xn[:, b, :]
                    last = dve.tensor_tensor(x[:, b, :], x[:, b, :], y, ALU.add)
                last.then_inc(x_ready, 1)

            def rotate(v, n, half, tb, at, tmp):
                c = cosT[:, tb, at:at + half].unsqueeze(1).to_broadcast([P, n, half])
                s_ = sinT[:, tb, at:at + half].unsqueeze(1).to_broadcast([P, n, half])
                t = [tmp[:, k, 0:n * half].rearrange("p (n h) -> p n h", n=n) for k in range(4)]
                x1, x2 = v[:, :, 0:half], v[:, :, half:2 * half]
                dve.tensor_tensor(t[0], x1, c, ALU.mult)
                dve.tensor_tensor(t[1], x2, s_, ALU.mult)
                dve.tensor_tensor(t[2], x2, c, ALU.mult)
                link(dve.tensor_tensor(t[3], x1, s_, ALU.mult))
                dve.tensor_tensor(x1, t[0], t[1], ALU.subtract)
                link(dve.tensor_tensor(x2, t[2], t[3], ALU.add))

            def angles():
                TWO_PI, MAGIC = 2 * np.pi, 1.5 * 2.0 ** 23
                c1 = 6.28125
                c2 = float(np.float32(np.round((TWO_PI - c1) * 2.0 ** 22) / 2.0 ** 22))
                c3 = float(np.float32(TWO_PI - c1 - c2))
                inv = col("inv")
                a = [ang[:, k].rearrange("p a b -> p (a b)") for k in range(4)]
                link(dve.tensor_copy(posf[:, :], pos[:, :]))
                for w, (lo, hi) in enumerate(((0, 16), (16, 24))):
                    for tb in range(TB):
                        last = dve.tensor_scalar(ang[:, 0, tb, lo:hi], inv[:, lo:hi],
                                                 posf[:, w * TB + tb:w * TB + tb + 1], None, ALU.mult)
                link(last)
                link(dve.tensor_scalar(a[1], a[0], float(1 / TWO_PI), MAGIC, ALU.mult, ALU.add))
                link(dve.tensor_scalar(a[2], a[1], MAGIC, None, ALU.subtract))
                for c in (c1, c2, c3):
                    link(dve.scalar_tensor_tensor(a[0], a[2], -c, a[0], ALU.mult, ALU.add))
                dve.tensor_scalar(a[1], a[0], 3.1415925, -3.1415925, ALU.min, ALU.max).then_inc(of("angle"), 1)
                dve.wait_ge(of("angle_abs"), 1)
                dve.tensor_scalar(a[3], a[2], -1.0, float(np.pi / 2), ALU.mult, ALU.add).then_inc(of("angle"), 1)
                dve.wait_ge(of("angle_sin"), 1)

            def attention(a, R):
                pairs, n0 = HEADS // 2, a * (HEADS // 2)
                scale = float(QD) ** -0.5 if a == 0 else 0.125
                neg = col("neg_causal" if a == 0 else "neg_window").unsqueeze(1).to_broadcast([P, 2, 384])

                def masked(j):
                    dve.wait_ge(of("att_s"), n0 + j + 1)
                    if j >= 2:
                        dve.wait_ge(of("att_p"), n0 + j - 1)
                    st, nm = R["st"][:, j % 2], R["nm"][:, j % 2].rearrange("p (e t) -> p e t", e=2)
                    link(dve.scalar_tensor_tensor(st, ps[:, 2:4, 0:384], scale, neg, ALU.mult, ALU.add))
                    dve.tensor_reduce(nm[:, :, 0:1], st[:, :, 0:P], AX.X, ALU.max, negate=True)
                    last = dve.tensor_reduce(nm[:, :, 1:2], st[:, :, P:384], AX.X, ALU.max, negate=True)
                    if a:
                        link(last)
                        sink = R["nsink"][:, 2 * j:2 * j + 2].unsqueeze(2).to_broadcast([P, 2, 2])
                        last = dve.tensor_tensor(nm, nm, sink, ALU.min)
                    last.then_inc(of("att_m"), 1)

                def normed(j):
                    dve.wait_ge(of("att_p"), n0 + j + 1)
                    su, p = R["su"][:, j % 2], R["p"][:, j % 2]
                    if a:
                        link(dve.tensor_tensor(su, su, R["es"][:, j % 2], ALU.add))
                    link(dve.reciprocal(R["rc"], su))
                    rc = R["rc"].rearrange("p (e t) -> p e t", e=2)
                    dve.tensor_tensor(p[:, :, 0:P], p[:, :, 0:P], rc[:, :, 0:1].to_broadcast([P, 2, P]), ALU.mult)
                    dve.tensor_tensor(p[:, :, P:384], p[:, :, P:384], rc[:, :, 1:2].to_broadcast([P, 2, T]),
                                      ALU.mult).then_inc(of("att_n"), 1)

                masked(0)
                for j in range(pairs):
                    if j + 1 < pairs:
                        masked(j + 1)
                    normed(j)
                    dve.wait_ge(of("att_av"), n0 + j + 1)
                    dve.tensor_copy(R["oT"][:, j, :], ps[:, 6 + j % 2, 0:T]).then_inc(of("att_o"), 1)

            def mla():
                norm_in("mla")
                R = attention_regions(0)
                rstd([(0, 2, 1.0 / QL, EPS), (2, 4, 1.0 / KVL, EPS)])
                for tb in range(TB):
                    dve.tensor_scalar(R["cn"][:, tb, 0:QL], R["mp"][:, tb, 0:QL], rs[:, tb:tb + 1], None, ALU.mult)
                    last = dve.tensor_scalar(R["cn"][:, tb, QL:QL + KVL], R["mp"][:, tb, QL:QL + KVL],
                                             rs[:, 2 + tb:3 + tb], None, ALU.mult)
                last.then_inc(of("mla_cn"), 1)
                for tb in range(TB):
                    kr = R["mp"][:, tb, QL + KVL:MLA_IN].unsqueeze(1)
                    rotate(kr, 1, 16, tb, 0, R["rot"])
                    dve.tensor_copy(split(R["k"][:, tb, :], HEADS, QD)[:, :, 64:QD], kr.to_broadcast([P, HEADS, ROPE]))
                dve.wait_ge(of("mla_q"), 1)
                for tb in range(TB):
                    rotate(split(R["q"][:, tb, :], HEADS, QD)[:, :, 64:QD], HEADS, 16, tb, 0, R["rot"])
                dve.wait_ge(used, AT["mla_ukv"] + 2)
                kv = bank(4, 4).rearrange("p (h c) -> p h c", h=HEADS)
                dve.tensor_copy(split(R["k"][:, 1, :], HEADS, QD)[:, :, 0:64], kv[:, :, 0:64])
                dve.tensor_copy(split(R["v"][:, 1, :], HEADS, 64), kv[:, :, 64:128]).then_inc(of("mla_kv_d"), 1)
                attention(0, R)
                add_normed(1.0)

            def swa():
                R = attention_regions(1)
                norm_in("kv")
                dve.wait_ge(used, AT["swa_kv"] + 2)
                for tb in range(TB):
                    last = dve.tensor_tensor(R["kv"][:, tb, :], ps[:, 4 + tb, 0:256], col("kv_b"), ALU.add)
                link(last)
                for tb in range(TB):
                    rotate(split(R["kv"][:, tb, 0:P], 2, 64)[:, :, 0:ROT], 2, ROT // 2, tb, 16, R["rot"])
                dve.tensor_scalar(R["nsink"], col("sinks"), -1.0, None, ALU.mult)
                for tb in range(TB):
                    for g in range(2):
                        last = dve.tensor_copy(split(R["kd"][:, tb, g, :], 2, 64),
                                               R["kv"][:, tb, g * 64:g * 64 + 64].unsqueeze(1).to_broadcast([P, 2, 64]))
                last.then_inc(of("swa_k"), 1)
                norm_in("swa")
                dve.wait_ge(used, AT["swa_q"] + KD)
                row_wait(0)
                for tb in range(TB):
                    last = dve.tensor_tensor(R["q"][:, tb, :], bank(2 * tb, 2), row[:, 0, :], ALU.add)
                link(last)
                for tb in range(TB):
                    rotate(split(R["q"][:, tb, :], HEADS, 64)[:, :, 0:ROT], HEADS, ROT // 2, tb, 16, R["rot"])
                link(dve.tensor_copy(R["rc"], R["nsink"][:, 0:4]))
                dve.tensor_copy(R["rc"], R["nsink"][:, 0:4]).then_inc(of("swa_q"), 1)
                attention(1, R)
                dve.wait_ge(used, AT["swa_out"] + KD)
                row_wait(1)
                add(row[:, 1, :])

            def ssm():
                R = ssm_regions()
                norm_in("ssm")
                conv = CAT["conv"][0]
                with dve.Fori(0, CONV_TILES // 4) as i:
                    for j in range(4):
                        dve.wait_ge(of("conv_acc"), i * 4 + (j + 1))
                        for k in range(3):
                            if k:
                                dve.wait_ge(of("conv_taps"), i * 12 + (3 * j + k))
                            d = k + 1
                            dve.scalar_tensor_tensor(R["acc"][:, j, d:T], ps[:, j, 0:T - d],
                                                     cols[:, bass.ds(i * 20 + (conv + 5 * j + 2 - k), 1)],
                                                     R["acc"][:, j, d:T], ALU.mult, ALU.add)\
                               .then_inc(of("conv_taps"), 1)
                two = [P, TB, SH]

                def heads(v):
                    return v.rearrange("p (c h) -> p c h", c=TB)

                dve.wait_ge(used, AT["ssm_dt"] + 1)
                dve.tensor_tensor(heads(R["u"]), heads(ps[:, 4, 0:64]), col("dt_bias").unsqueeze(1).to_broadcast(two),
                                  ALU.add).then_inc(of("ssm_u"), 1)
                dve.wait_ge(of("ssm_l"), 1)
                link(dve.scalar_tensor_tensor(R["dt"], R["u"], 0.0, R["lz"], ALU.max, ALU.add))
                dve.scalar_tensor_tensor(heads(R["a"]), heads(R["dt"]), -1.0,
                                         R["eA"].unsqueeze(1).to_broadcast(two), ALU.mult, ALU.mult)\
                   .then_inc(of("ssm_a"), 1)
                dve.wait_ge(of("ssm_cs"), 1)
                link(dve.tensor_copy(R["acs"], ps[:, 5, 0:64]))
                dve.tensor_tensor(R["de"], ps[:, 5, 64:128], R["acs"], ALU.subtract).then_inc(of("ssm_de"), 1)
                for n in range(8):
                    dve.wait_ge(of("ssm_xs"), n + 1)
                    tb, m = n % 2, n // 2
                    last = dve.tensor_tensor(split(R["X"][:, tb, m * 512:(m + 1) * 512], 8, 64),
                                             split(R["xs"][:, tb, m * 512:(m + 1) * 512], 8, 64),
                                             R["dt"][:, tb * SH + 8 * m:tb * SH + 8 * m + 8].unsqueeze(2)
                                             .to_broadcast([P, 8, 64]), ALU.mult)
                link(last)
                dve.wait_ge(of("ssm_ex"), 1)

                def per_head(v, c, g):
                    o = c * SH + HPG * g
                    return v[:, o:o + HPG].unsqueeze(2).to_broadcast([P, HPG, 64])

                def spread(n):
                    g, c = n // 2, n % 2
                    if n >= 2:
                        dve.wait_ge(of("sg_cb"), n - 1)
                    o = c * SH + HPG * g
                    dve.tensor_tensor(R["ta"][:, n % 2], col("up_incl").unsqueeze(1).to_broadcast([P, HPG, P]),
                                      R["a"][:, o:o + HPG].unsqueeze(2).to_broadcast([P, HPG, P]), ALU.mult)\
                       .then_inc(of("sg_ta"), 1)

                def outputs(n):
                    g, c = n // 2, n % 2
                    o = slice(g * T, (g + 1) * T)
                    t = R["t"]
                    if n:
                        dve.wait_ge(of("sg_done"), n)
                    link(dve.tensor_tensor(split(t[:, 0], HPG, 64), split(R["xs"][:, c, o], HPG, 64),
                                           col("d_skip")[:, HPG * g:HPG * g + HPG].unsqueeze(2)
                                           .to_broadcast([P, HPG, 64]), ALU.mult))
                    dve.wait_ge(of("sg_y"), n + 1)
                    if c:
                        link(dve.tensor_tensor(split(t[:, 1], HPG, 64), split(ps[:, 4 + n % 2, T:2 * T], HPG, 64),
                                               per_head(R["eacs"], c, g), ALU.mult))
                        link(dve.tensor_tensor(t[:, 0], t[:, 0], t[:, 1], ALU.add))
                    dve.tensor_tensor(t[:, 0], t[:, 0], ps[:, 4 + n % 2, 0:T], ALU.add).then_inc(of("sg_o"), 1)
                    dve.wait_ge(of("sg_o"), n + 1)
                    dve.tensor_tensor(R["zs"][:, c, o], R["zs"][:, c, o], t[:, 0], ALU.mult)\
                       .then_inc(of("sg_done"), 1)

                spread(0)
                for n in range(2 * SG):
                    g, c = n // 2, n % 2
                    if n + 1 < 2 * SG:
                        spread(n + 1)
                    dve.wait_ge(of("sg_cb"), n + 1)
                    if n >= 2:
                        dve.wait_ge(of("sg_L"), n - 1)
                    for q in range(HPG):
                        o = c * SH + HPG * g + q
                        last = dve.scalar_tensor_tensor(R["seg"][:, n % 2, q, :], ps[:, n % 2, q * P:(q + 1) * P],
                                                        R["acs"][:, o:o + 1], col("neg_after"),
                                                        ALU.subtract, ALU.add)
                    last.then_inc(of("sg_seg"), 1)
                    if n:
                        outputs(n - 1)
                    if n >= 2:
                        dve.wait_ge(of("sg_y"), n - 1)
                    if c == 0:
                        link(dve.tensor_tensor(split(R["Xd"][:, g % 2, :], HPG, 64),
                                               split(R["X"][:, 0, g * T:(g + 1) * T], HPG, 64),
                                               per_head(R["dte"], 0, g), ALU.mult))
                    dve.wait_ge(of("sg_L"), n + 1)
                    dve.tensor_tensor(R["M"][:, n % 2], R["L"][:, n % 2],
                                      ps[:, 2 + n % 2, 0:P].unsqueeze(1).to_broadcast([P, HPG, P]), ALU.mult)\
                       .then_inc(of("sg_M"), 1)
                outputs(2 * SG - 1)
                rstd([(0, 16, 1.0 / T, 1e-5)])
                for tb in range(TB):
                    v = split(R["zs"][:, tb, :], SG, T)
                    dve.tensor_tensor(v, v, rs[:, tb * SG:(tb + 1) * SG].unsqueeze(2).to_broadcast([P, SG, T]),
                                      ALU.mult).then_inc(of("ssm_yn"), 1)
                for k in (2, 3, 6, 7, 10, 11, 14, 15):
                    dve.wait_ge(of("ssm_yT"), k // 2 + 1)
                    dve.tensor_scalar(R["yT"][:, k, :], ps[:, k // 2, (k % 2) * T:(k % 2 + 1) * T],
                                      col("gate_norm")[:, k:k + 1], None, ALU.mult).then_inc(of("ssm_yT_d"), 1)
                dve.wait_ge(used, AT["ssm_out"] + DI // P)
                add()

            def top16(src, spare, values, indices):
                both = range(TB)
                for b in both:
                    last = dve.max(values(b, 0), src(b))
                link(last)
                for b in both:
                    dve.max_index(indices(b, 0), values(b, 0), src(b))
                    last = dve.match_replace(spare(b), values(b, 0), src(b), -3.0e38)
                link(last)
                for b in both:
                    last = dve.max(values(b, 8), spare(b))
                link(last)
                for b in both:
                    last = dve.max_index(indices(b, 8), values(b, 8), spare(b))
                return last

            def peer(l):
                R = peer_regions()
                norm_in(f"peer{l}")
                n0 = SUBS * l
                si = R["si"].bitcast(U32)
                for m in range(SUBS):
                    dve.wait_ge(of("peer_sp"), n0 + m + 1)
                    dve.tensor_copy(R["s"][:, :, m, :], ps[:, 2 + m % 2, 0:T].rearrange("p (b k) -> p b k", b=TB))\
                       .then_inc(of("peer_s"), 1)
                    dve.wait_ge(of("peer_s"), n0 + m + 1)
                    link(top16(lambda b: R["s"][:, b, m, :], lambda b: R["s2"][:, b, :],
                               lambda b, o: R["sv"][:, b, m, o:o + 8], lambda b, o: si[:, b, m, o:o + 8]))
                link(dve.tensor_copy(R["sif"], si))
                bp = R["bp"].bitcast(U32)
                bp3 = bp.rearrange("p (b h k) -> p b h k", b=TB, h=PH)
                for h in range(PH):
                    for b in range(TB):
                        last = dve.tensor_tensor(split(R["cand"][:, b, :], TOPK, TOPK),
                                                 R["sv"][:, b, 2 * h, :].unsqueeze(2).to_broadcast([P, TOPK, TOPK]),
                                                 R["sv"][:, b, 2 * h + 1, :].unsqueeze(1).to_broadcast([P, TOPK, TOPK]),
                                                 ALU.add)
                    link(last)
                    link(top16(lambda b: R["cand"][:, b, :], lambda b: R["cand2"][:, b, :],
                               lambda b, o: R["bs"][:, b, h, o:o + 8], lambda b, o: bp3[:, b, h, o:o + 8]))
                n = TB * PH
                bs3 = R["bs"].rearrange("p b h k -> p (b h) k")
                e3 = R["e"].rearrange("p b h k -> p (b h) k")
                dve.tensor_tensor(e3, bs3, bs3[:, :, 0:1].to_broadcast([P, n, TOPK]), ALU.subtract)\
                   .then_inc(of("peer_e"), 1)
                pa = R["pa"].bitcast(U32)
                dve.tensor_scalar(pa[:, 0, :], bp, 4, None, ALU.logical_shift_right)
                link(dve.tensor_scalar(pa[:, 1, :], bp, 15, None, ALU.bitwise_and))
                link(dve.tensor_copy(R["pf"].rearrange("p c b h k -> p c (b h k)"), pa))
                full = [P, PH, TOPK, TOPK]
                iota = col("iota")[:, 0:TOPK].unsqueeze(1).unsqueeze(1).to_broadcast(full)
                for b in range(TB):
                    keys = R["sif"][:, b].rearrange("p (h c) a -> p h c a", c=2)
                    for c in range(2):
                        link(dve.tensor_tensor(R["eq"], R["pf"][:, c, b].unsqueeze(3).to_broadcast(full), iota,
                                               ALU.is_equal))
                        link(dve.tensor_tensor(R["eq"], R["eq"], keys[:, :, c, :].unsqueeze(2).to_broadcast(full),
                                               ALU.mult))
                        link(dve.tensor_reduce(split(R["pk"][:, c, b, :], PH, TOPK).unsqueeze(3), R["eq"], AX.X,
                                               ALU.add))
                dve.wait_ge(of("peer_ex"), l + 1)
                link(dve.tensor_reduce(R["sum"].unsqueeze(2), e3, AX.X, ALU.add))
                link(dve.reciprocal(R["rc"], R["sum"]))
                dve.tensor_tensor(R["pk"][:, 2].rearrange("p b (h k) -> p (b h) k", h=PH), e3,
                                  R["rc"].unsqueeze(2).to_broadcast([P, n, TOPK]), ALU.mult).then_inc(of("picks"), 1)
                n0 = 64 * l
                dve.wait_ge(of("picksTs"), l + 1)
                dve.wait_ge(of("gelu"), n0 + 64)
                iota4 = col("iota").unsqueeze(1).to_broadcast([P, 4, P])

                def hot(n, i=None):
                    t = 4 * n if i is None else i * 16 + 4 * n
                    if n >= 2:
                        g = n0 + n - 1
                        dve.wait_ge(of("gates"), g if i is None else i * 4 + g)
                    dve.tensor_tensor(R["hot"][:, n % 2, 0], iota4,
                                      pick[:, 0, bass.ds(t, 4)].unsqueeze(2).to_broadcast([P, 4, P]), ALU.is_equal)
                    dve.tensor_tensor(R["hot"][:, n % 2, 1], iota4,
                                      pick[:, 1, bass.ds(t, 4)].unsqueeze(2).to_broadcast([P, 4, P]), ALU.is_equal)\
                       .then_inc(of("hot1"), 1)
                    g = n0 + n + 1
                    dve.wait_ge(of("hot1"), g if i is None else i * 4 + g)
                    dve.tensor_tensor(R["hot"][:, n % 2, 1], R["hot"][:, n % 2, 1],
                                      pick[:, 2, bass.ds(t, 4)].unsqueeze(2).to_broadcast([P, 4, P]), ALU.mult)\
                       .then_inc(of("hot"), 1)

                def gated(n, i=None):
                    t = 4 * n if i is None else i * 16 + 4 * n
                    g = n0 + n + 1
                    dve.wait_ge(of("gates"), g if i is None else i * 4 + g)
                    w = R["A"][:, :, bass.ds(t, 4)].rearrange("p i t -> p t i")
                    dve.tensor_tensor(w, w, ps[:, n % 4, :].rearrange("p (t i) -> p t i", t=4), ALU.mult)\
                       .then_inc(of("gated"), 1)

                hot(0)
                hot(1)
                gated(0)
                hot(2)
                gated(1)
                with dve.Fori(0, 15) as i:
                    for n in range(3, 7):
                        hot(n, i)
                        gated(n - 1, i)
                hot(63)
                gated(62)
                gated(63)
                dve.wait_ge(used, AT[f"peer{l}_v"] + KEYS)
                add()

            def ple(l):
                norm_in(f"ple{l}")
                sg = region(ARENA, TB, D)[0]
                dve.wait_ge(of("ple_gate"), l + 1)
                dve.wait_ge(used, AT[f"ple{l}_proj"] + 2)
                for b in range(TB):
                    link(dve.tensor_tensor(xn[:, b, :], sg[:, b, :], bank(4 + 2 * b, 2), ALU.mult))
                    last = dve.tensor_tensor(x[:, b, :], x[:, b, :], xn[:, b, :], ALU.add)
                last.then_inc(x_ready, 1)


            link(dve.memset(ms[:, :], 1.0))
            dve.wait_ge(pos_loaded, 16)
            dve.wait_ge(cols_loaded, 16)
            dve.wait_ge(x_loaded, 16)
            angles()
            fs = 0
            for name in layers:
                if name.startswith("ffn"):
                    ffn(fs, name)
                    fs += 1
                elif name == "sb":
                    stick_breaking()
                elif name in ("mla", "swa", "ssm"):
                    {"mla": mla, "swa": swa, "ssm": ssm}[name]()
                elif name.startswith("peer"):
                    peer(int(name[-1]))
                elif name.startswith("ple"):
                    ple(int(name[-1]))
            if stop == len(LAYERS):
                rstd([(0, TB, 1.0 / D, EPS)])
                row_wait(0)
                for b in range(TB):
                    dve.scalar_tensor_tensor(xn[:, b, :], x[:, b, :], rs[:, b:b + 1], row[:, 0, :],
                                             ALU.mult, ALU.mult).then_inc(of("result"), 1)
            else:
                dve.wait_ge(x_ready, stop)
                for b in range(TB):
                    dve.tensor_copy(xn[:, b, :], x[:, b, :]).then_inc(of("result"), 1)
            n_stats[0] = stats[0]

        @block.gpsimd
        def _(pool):
            pool.wait_ge(cols_loaded, 16)
            with pool.Fori(0, n_stats[0]) as i:
                pool.wait_ge(ms_ready, i + 1)
                pool.tensor_tensor(rs[:, :], ms[:, :], col("nhalf"), ALU.pow).then_inc(rs_ready, 1)


def by_rows(w):
    return w.reshape(-1, P, w.shape[-1])


def by_columns(w):
    return w.reshape(KD, P, -1, P).transpose(2, 1, 0, 3).reshape(-1, P, KD * P)


def padded(w):
    full = np.zeros((w.shape[0], P, BLK), w.dtype)
    full[:, :, :w.shape[2]] = w
    return full


def grouped(w, n):
    c = w.shape[1]
    w = w.reshape(-1, n, P, c).transpose(0, 2, 1, 3)
    return w.reshape(-1, P, n * c)


def feed_forward(w_in, w_out):
    cols, down = by_columns(w_in), by_rows(w_out)
    gate, up = cols[:FC], cols[FC:]
    out = [gate[0:1], up[0:1]]
    both = np.stack([gate[1:], up[1:], down[:-1]], 1).reshape(-1, P, BLK)
    return out + [both, down[-1:]]


def weight_stream(a):
    ffn = [feed_forward(a["ffn_w_in"][i, j], a["ffn_w_out"][i, j]) for i in range(2) for j in range(2)]
    qkv = by_columns(a["sb_w_in"][0]).reshape(3, KD, P, BLK).transpose(1, 0, 2, 3).reshape(-1, P, BLK)
    uq = a["mla_w_uq"][0].reshape(2, P, 3, 512).transpose(2, 1, 0, 3).reshape(3, P, BLK)
    ukv = a["mla_w_ukv"][0].reshape(P, 2, BLK).transpose(1, 0, 2)
    ssm = a["ssm_in_w_2"][0]
    z = ssm[:, :DI].reshape(KD, P, 2, D).transpose(2, 0, 1, 3).reshape(16, P, D)

    def peer(i):
        u = a["peer_u_2"][i].reshape(KEYS, KEYS, KD, P).transpose(1, 3, 2, 0).reshape(KEYS, P, BLK)
        v = a["peer_v_2"][i].reshape(KEYS, KEYS, D).transpose(1, 0, 2)
        return [by_columns(a["peer_q_w_2"][i]), u, v, by_rows(a["ple_gate_w_2"][i]), by_rows(a["ple_proj_2"][i])]

    parts = ffn[0] + [qkv, by_rows(a["sb_w_out"][0])] + ffn[1] + ffn[2]
    parts += [padded(grouped(a["mla_w_in"][0], 2)), uq, ukv, by_rows(a["mla_w_out"][0])] + ffn[3]
    parts += [z, by_columns(ssm[:, DI:DI + CONV_TILES * P]), padded(grouped(ssm[:, DI + CONV_TILES * P:], KD)),
              by_rows(a["ssm_out_w_2"][0])]
    parts += peer(0) + [grouped(a["kv_w_2"], 4), by_rows(a["q_w_2"][0]), by_rows(a["o_w_2"][0])] + peer(1)
    return np.concatenate(parts)


def columns(a):
    i, j = np.arange(P)[:, None], np.arange(P)[None, :]
    f = np.float32

    def tall(v):
        return np.asarray(v).reshape(-1, P).T

    def wide(v):
        return np.broadcast_to(np.asarray(v).reshape(1, -1), (P, np.asarray(v).size))

    neg = f(NEG)
    causal = np.where(j <= i, f(0), neg)
    after = np.where(i <= j, f(0), neg)
    inv1 = np.power(10000.0, (-np.arange(0, ROPE, 2, dtype=f) / f(ROPE)).astype(np.float64)).astype(f)
    inv2 = np.power(500000.0, (-np.arange(0, ROT, 2, dtype=f) / f(ROT)).astype(np.float64)).astype(f)
    g, ng = a["norm_g"], np.concatenate
    gains = [g[0, 0], g[0, 2], g[0, 4], g[1, 0], g[1, 2], g[1, 4], a["ssm_norm_2"][0], a["peer_norm_2"][0],
             a["ple_norm_2"][0], a["kv_norm_2"], a["attn_norm_2"][0], a["peer_norm_2"][1], a["ple_norm_2"][1]]
    conv = ng([a["ssm_conv_w_2"][0], a["ssm_conv_b_2"]]).reshape(5, CONV_TILES, P).transpose(2, 1, 0)
    subkeys = a["peer_sub_keys_2"].transpose(3, 0, 1, 2).reshape(P, -1)
    pT = a["p_2"].reshape(2, T, 2, P).transpose(3, 0, 2, 1).reshape(P, -1)
    parts = {"ident": i == j, "up_incl": i <= j, "lo_incl": i >= j, "up_strict": i < j,
             "neg_strict": np.where(i < j, f(0), neg), "neg_causal": ng([causal, np.zeros((P, P), f), causal], 1),
             "neg_window": ng([causal, np.where(j > i, f(0), neg), causal], 1), "neg_after": after,
             "ones": np.ones((P, P)), "iota": wide(np.arange(P)), "inv": wide(ng([inv1, inv2])),
             "nhalf": np.full((P, 16), -0.5), "gains": ng([tall(v) for v in gains], 1),
             "gate_norm": tall(a["ssm_gate_norm_2"]), "q_norm": tall(a["mla_q_norm"]),
             "kv_norm": tall(a["mla_kv_norm"]), "conv": conv.reshape(P, -1), "subkeys": subkeys,
             "dt_bias": wide(a["ssm_dt_bias_2"]), "a_log": wide(a["ssm_A_log_2"]), "d_skip": wide(a["ssm_D_2"]),
             "sinks": wide(a["sinks_2"]), "kv_b": wide(a["kv_b_2"]), "pT": pT}
    return ng([np.asarray(parts[name], f) for name, _ in COLS], 1)


def laid_out(inputs):
    a = {k: np.asarray(v) for k, v in inputs.items()}
    g = a["norm_g"]
    pos = np.stack([a["positions"][0].reshape(TB, P), a["positions_2"][0].reshape(TB, P)]).transpose(2, 0, 1)
    rows = np.stack([g[0, 1], g[0, 3], g[0, 5], g[1, 1], g[1, 3], g[1, 5], a["q_b_2"][0], a["final_norm_2"],
                     a["o_b_2"][0]])
    return {"stream": weight_stream(a), "x_in": np.ascontiguousarray(a["x"][0]),
            "pos_in": np.ascontiguousarray(pos.reshape(P, 2 * TB).astype(np.int32)),
            "cols_in": np.ascontiguousarray(columns(a)), "rows_in": rows}


def kernel(**inputs):
    import concourse.bacc as bacc
    from concourse.bass_utils import run_bass_kernel_spmd

    arrays = laid_out(inputs)
    nc = bacc.Bacc("TRN2", target_bir_lowering=False, num_devices=1)
    args = [nc.dram_tensor(name, a.shape, mybir.dt.from_np(a.dtype), kind="ExternalInput").ap()
            for name, a in arrays.items()]
    out = nc.dram_tensor("out", (T, D), F32, kind="ExternalOutput").ap()
    build_program(nc, *args, out)
    r = run_bass_kernel_spmd(nc, [arrays], core_ids=[0])
    return r.results[0]["out"].reshape(1, T, D)
```

```python
import concourse.bass as bass
from concourse import mybir
from contextlib import ExitStack
import numpy as np

F32 = mybir.dt.float32
F32R = mybir.dt.float32r
U32 = mybir.dt.uint32
I32 = mybir.dt.int32
ACT = mybir.ActivationFunctionType
ALU = mybir.AluOpType
AX = mybir.AxisListType

P = 128
D = 1024
T = 256
TB = T // P
KD = D // P
FF = 2816
FC = FF // P
HEADS = 16
QL, KVL, ROPE, NOPE = 256, 128, 32, 64
MLA_IN = QL + KVL + ROPE
QD = NOPE + ROPE
DI = 2048
SH, SG, SN, SP_ = 32, 8, 128, 64
HPG = SH // SG
CONV_TILES = (DI + 2 * SG * SN) // P
KEYS = 128
TOPK = 16
PH = 8
SUBS = 2 * PH
ROT = 16
NEG = -1.0e30
EPS = 1e-6

BLK = 1024
RING = 4
LAYERS = ["ffn0", "sb", "ffn1", "ffn2", "mla", "ffn3", "ssm", "peer0", "ple0", "swa", "peer1", "ple1"]
PARTS = [("ffn0", 3 * FC), ("sb_qkv", 24), ("sb_out", 8), ("ffn1", 3 * FC), ("ffn2", 3 * FC),
         ("mla_in", 4), ("mla_uq", 3), ("mla_ukv", 2), ("mla_out", 8), ("ffn3", 3 * FC),
         ("ssm_z", 16), ("ssm_xbc", CONV_TILES), ("ssm_dt", 1), ("ssm_out", 16),
         ("peer0_q", SUBS), ("peer0_u", KEYS), ("peer0_v", KEYS), ("ple0_gate", 8), ("ple0_proj", 2),
         ("swa_kv", 2), ("swa_q", 8), ("swa_out", 8),
         ("peer1_q", SUBS), ("peer1_u", KEYS), ("peer1_v", KEYS), ("ple1_gate", 8), ("ple1_proj", 2)]


def first_blocks():
    at, n = {}, 0
    for name, count in PARTS:
        at[name] = n
        n += count
    at["end"] = n
    return at


AT = first_blocks()
SLOTS = 4


FIRST_PART = {"ffn0": "ffn0", "sb": "sb_qkv", "ffn1": "ffn1", "ffn2": "ffn2", "mla": "mla_in", "ffn3": "ffn3",
              "ssm": "ssm_z", "peer0": "peer0_q", "ple0": "ple0_gate", "kv": "swa_kv", "peer1": "peer1_q",
              "ple1": "ple1_gate"}
SPLIT_PARTS = ["ffn0", "sb_qkv", "ffn1", "ffn2", "mla_in", "ffn3", "ssm_z", "ssm_xbc", "ssm_dt", "peer0_q",
               "peer0_u", "peer0_v", "ple0_gate", "swa_kv", "swa_q", "peer1_q", "peer1_u", "peer1_v", "ple1_gate"]
POOL_BLOCKS = {"sb": 24, "mla": 4, "ssm": 16 + CONV_TILES + 1, "peer0": SUBS + KEYS + SLOTS, "ple0": 8,
               "kv": 10, "peer1": SUBS + KEYS + SLOTS, "ple1": 8}


def split_blocks():
    of_block, made = {}, {"dve": 0, "pool": 0}
    for name, count in PARTS:
        for n in range(count if name in SPLIT_PARTS else 0):
            who = "dve" if name.startswith("ffn") or (name[-2:] == "_v" and n >= SLOTS) else "pool"
            of_block[AT[name] + n] = (len(of_block), who, made[who])
            made[who] += 1
    return of_block


SPLIT = split_blocks()

COLS = [("ident", P), ("up_incl", P), ("lo_incl", P), ("ones", P), ("iota", P),
        ("inv", 24), ("nhalf", 16), ("gains", 13 * KD), ("gate_norm", DI // P), ("q_norm", 2), ("kv_norm", 1),
        ("conv", CONV_TILES * 5), ("subkeys", 2 * 2 * KEYS), ("dt_bias", SH), ("a_log", SH), ("d_skip", SH),
        ("sinks", HEADS), ("kv_b", 256)]
OWN_COLS = [("up_strict", P), ("neg_strict", P), ("neg_causal", 3 * P), ("neg_window", 3 * P), ("neg_after", P),
            ("pT0", 2 * T), ("pT1", 2 * T)]
OWN_OF = {"sb": ("up_strict", 2 * P), "mla": ("neg_causal", 3 * P), "swa": ("neg_window", 3 * P),
          "ssm": ("neg_after", P), "ple0": ("pT0", 2 * T), "ple1": ("pT1", 2 * T)}


def col_offsets():
    at, n = {}, 0
    for name, width in COLS:
        at[name] = (n, width)
        n += width
    at["end"] = (n, 0)
    for name, width in OWN_COLS:
        at[name] = (n, width)
        n += width
    return at


CAT = col_offsets()
NCOLS = CAT["end"][0]
ROWS = 9

NORM_OF = {"ffn0": 0, "sb": 1, "ffn1": 2, "ffn2": 3, "mla": 4, "ffn3": 5, "ssm": 6, "peer0": 7, "ple0": 8,
           "kv": 9, "swa": 10, "peer1": 11, "ple1": 12}


def build_program(nc, stream, x_in, pos_in, cols_in, rows_in, out):
    n_blocks = AT["end"]
    ctx = ExitStack()
    with ctx:
        def sb(name, shape, dt=F32):
            return ctx.enter_context(nc.sbuf_tensor(name, shape, dt))

        def sem(name):
            return ctx.enter_context(nc.semaphore(name))

        x = sb("x", [P, TB, D])
        hT_hi, hT_lo = sb("hT_hi", [P, KD, T], F32R), sb("hT_lo", [P, KD, T], F32R)
        ring = sb("ring", [P, RING, BLK])
        ring_hi = sb("ring_hi", [P, SLOTS, BLK], F32R)
        ring_lo = sb("ring_lo", [P, SLOTS, BLK], F32R)
        w_hi = sb("w_hi", [P, 2, T], F32R)
        w_lo = sb("w_lo", [P, 2, T], F32R)
        cols = sb("cols", [P, NCOLS])
        row = sb("row", [P, 2, D])
        arena = sb("arena", [P, KEYS * T])
        pick = sb("pick", [P, 3, T])
        ss = sb("ss", [P, 16])
        ms = sb("ms", [P, 16])
        rs = sb("rs", [P, 16])
        pos = sb("pos", [P, 2 * TB], I32)
        posf = sb("posf", [P, 2 * TB])
        ang = sb("ang", [P, 4, TB, 24])
        cosT = sb("cosT", [P, TB, 24])
        sinT = sb("sinT", [P, TB, 24])
        ps = ctx.enter_context(nc.psum_tensor("ps", [P, 8, 512], F32))

        def col(name, *dims):
            o, w = CAT[name]
            a = cols[:, o:o + w]
            return split(a, *dims) if dims else a

        def split(a, *dims):
            if len(dims) == 1:
                return a
            names = "abcd"[:len(dims)]
            return a.rearrange(f"p ({' '.join(names)}) -> p {' '.join(names)}",
                               **{n: d for n, d in zip(names[1:], dims[1:])})

        def region(at, *dims):
            n = 1
            for d in dims:
                n *= d
            return split(arena[:, at:at + n], *dims), at + n

        def gain(v, k):
            o = CAT["gains"][0] + v * KD + k
            return cols[:, o:o + 1]

        loaded = [sem(f"block_loaded{i}") for i in range(RING)]
        used = sem("blocks_used")
        hi_ready = sem("block_hi_ready")
        lo_ready = {"dve": sem("block_lo_by_dve"), "pool": sem("block_lo_by_pool")}
        own_loaded = sem("own_cols_loaded")
        x_loaded, cols_loaded, pos_loaded = sem("x_loaded"), sem("cols_loaded"), sem("pos_loaded")
        row_loaded = [sem("row_loaded0"), sem("row_loaded1")]
        x_ready = sem("x_ready")
        x_first = sem("x_first_tile")
        first_squared = sem("first_squared")
        ss_ready, ms_ready, rs_ready = sem("ss_ready"), sem("ms_ready"), sem("rs_ready")
        xn_ready = sem("xn_ready")
        xT_ready = sem("xT_ready")
        hT_a, hT_d = sem("hT_by_act"), sem("hT_by_dve")
        silu_ready, hidden_ready = sem("silu_ready"), sem("hidden_ready")
        dve_chain, act_chain = sem("dve_chain"), sem("act_chain")
        out_done = sem("out_done")
        xn, _ = region(0, TB, D)
        ARENA = TB * D
        S = {}

        def of(name):
            if name not in S:
                S[name] = sem(name)
            return S[name]

        n_stats = [0]
        stats_before = {}

        def sb_regions():
            r, at = {}, ARENA
            for name, dims in (("own", (2, P)), ("q", (2, T)), ("k", (2, T)), ("v", (2, TB, P)), ("z", (2, 384)), ("az", (2, 384)),
                               ("ez", (2, 384)), ("lz", (2, 384)), ("sp", (2, 512)), ("t", (2, 384)),
                               ("a", (2, 384)), ("oT", (KD, T))):
                r[name], at = region(at, *dims)
            return r

        def places(at, *wanted):
            r = {}
            for name, dims in wanted:
                r[name], at = region(at, *dims)
            assert at <= KEYS * T
            return r

        def own_columns(name):
            return arena[:, ARENA:ARENA + OWN_OF[name][1]]

        def attention_regions(a):
            own = ([("mp", (TB, MLA_IN)), ("cn", (TB, QL + KVL)), ("cT", (3, T)), ("q", (TB, HEADS * QD)),
                    ("k", (TB, HEADS * QD)), ("v", (TB, HEADS * 64)), ("qkT", (2, 2, 512))] if a == 0 else
                   [("kv", (TB, 256)), ("kd", (TB, 2, P)), ("kT", (2, T)), ("q", (TB, D)), ("qT", (2, T)),
                    ("nsink", (HEADS,)), ("es", (2, 4))])
            return places(ARENA, ("own", (3 * P,)), *own, ("st", (2, 2, 384)), ("p", (2, 2, 384)), ("pT", (2, 384)), ("nm", (2, 4)),
                          ("su", (2, 4)), ("rc", (4,)), ("oT", (KD, T)), ("rot", (4, HEADS * 16)))

        def ssm_regions():
            r = places(ARENA, ("own", (P,)), ("zs", (TB, DI)), ("xc", (CONV_TILES, T)), ("xs", (TB, DI)),
                       ("Bl", (SG, P)), ("ta", (2, HPG, P)), ("seg", (2, HPG, P)), ("L", (2, HPG, P)),
                       ("M", (2, HPG, P)), ("Xd", (2, T)), ("st", (2, T)), ("t", (2, T)), ("acc", (4, T)),
                       ("u", (64,)), ("az", (64,)), ("ez", (64,)), ("lz", (64,)), ("dt", (64,)), ("a", (64,)),
                       ("acs", (64,)), ("de", (64,)), ("dte", (64,)), ("eacs", (64,)), ("eA", (SH,)),
                       ("X", (TB, DI)))
            r["yT"] = r["xc"]
            return r

        HOT_BY_DVE = 1
        LATE = 88

        def peer_regions():
            r = places(LATE * T, ("s", (TB, SUBS, KEYS)), ("s2", (TB, KEYS)), ("sv", (TB, SUBS, TOPK)),
                       ("si", (TB, SUBS, TOPK)), ("sif", (TB, SUBS, TOPK)), ("cand", (TB, 256)),
                       ("cand2", (TB, 256)), ("bs", (TB, PH, TOPK)), ("bp", (TB * PH * TOPK,)),
                       ("pa", (2, TB * PH * TOPK)), ("pf", (2, TB, PH, TOPK)), ("e", (TB, PH, TOPK)),
                       ("sum", (TB * PH,)), ("rc", (TB * PH,)))
            r["pk"] = split(row[:, :, :].rearrange("p a b -> p (a b)")[:, 0:3 * TB * P], 3, TB, P)
            r["eq"] = split(r["s"][:, 0].rearrange("p m k -> p (m k)"), PH, TOPK, TOPK)
            r["A"] = arena[:, :].rearrange("p (i t) -> p i t", t=T)
            r["hot"] = row[:, :, :].rearrange("p a b -> p (a b)").rearrange("p (s c t k) -> p s c t k", s=2, c=2, t=4)
            r["qT"] = pick[:, 0:2, :]
            return r

        block = ctx.enter_context(nc.Block())

        def wait_loaded(e, b, i=None, per_turn=0):
            v = 16 * (b // RING + 1)
            e.wait_ge(loaded[b % RING], v if i is None else i * (16 * per_turn // RING) + v)

        def count(v, i=None, per_turn=0):
            return v if i is None else i * per_turn + v

        def make_hi(act, b, i=None, per_turn=0):
            wait_loaded(act, b, i, per_turn)
            if b >= SLOTS:
                act.wait_ge(used, count(b - SLOTS + 1, i, per_turn))
            act.activation(ring_hi[:, b % SLOTS, :], ring[:, b % RING, :], ACT.Copy).then_inc(hi_ready, 1)

        def make_lo(e, b, i=None, per_turn=0):
            n, who, own = SPLIT[b]
            e.wait_ge(hi_ready, count(n + 1, i, per_turn))
            e.tensor_tensor(ring_lo[:, b % SLOTS, :], ring[:, b % RING, :], ring_hi[:, b % SLOTS, :].bitcast(F32),
                            ALU.subtract).then_inc(lo_ready[who], 1)

        def wait_split(e, b, i=None, per_turn=0):
            n, who, own = SPLIT[b]
            e.wait_ge(lo_ready[who], count(own + 1, i, per_turn))

        hT_by = {0: 0}
        for v_, name in enumerate(["ffn0", "sb", "ffn1", "ffn2", "mla", "ffn3", "ssm", "peer0", "ple0", "kv", "swa",
                                   "peer1", "ple1"]):
            hT_by[v_ + 1] = hT_by[v_] + KD

        def bank(k, n=1):
            return ps[:, k:k + n, :].rearrange("p a b -> p (a b)")

        def link_for(engine, chain):
            n = [0]

            def link(ins):
                n[0] += 1
                ins.then_inc(chain, 1)
                engine.wait_ge(chain, n[0])
            return link

        x_of = {}
        for n, name in enumerate(LAYERS):
            x_of[name] = n
        x_of["kv"] = x_of["swa"]

        def gated_tile(R, j, i=None):
            return R["A"][:, j, :] if i is None else \
                R["A"][:, bass.ds(i * 4 + j, 1), :].rearrange("p a t -> p (a t)")

        def hot_loop(engine, hot):
            hot(0)
            hot(1)
            with engine.Fori(0, 15) as i:
                for n in range(2, 6):
                    hot(n, i)
            hot(62)
            hot(63)

        def own_before(name):
            return sum(n in OWN_OF for n in LAYERS[:LAYERS.index(name)])

        @block.sync
        def _(sp):
            sp.dma_start(x[:, :, :], x_in.rearrange("(b p) d -> p b d", p=P)).then_inc(x_loaded, 16)
            sp.dma_start(cols[:, :], cols_in[:, 0:NCOLS]).then_inc(cols_loaded, 16)
            sp.dma_start(pos[:, :], pos_in).then_inc(pos_loaded, 16)
            for j in range(RING):
                sp.dma_start(ring[:, j, :], stream[j]).then_inc(loaded[j], 16)
            b = RING
            while b < n_blocks:
                way = SPLIT.get(b - RING, (0, "used"))[1]
                end = b
                while end < n_blocks and SPLIT.get(end - RING, (0, "used"))[1] == way:
                    end += 1
                first = b - RING + 1 if way == "used" else SPLIT[b - RING][2] + 1
                free = used if way == "used" else lo_ready[way]
                turns = (end - b) // RING
                if turns < 2:
                    turns = 0
                else:
                    with sp.Fori(0, turns) as i:
                        for j in range(RING):
                            sp.wait_ge(free, i * RING + (first + j))
                            sp.dma_start(ring[:, (b + j) % RING, :], stream[bass.ds(i * RING + (b + j), 1)]
                                         .rearrange("a p n -> (a p) n")).then_inc(loaded[(b + j) % RING], 16)
                for j in range(turns * RING, end - b):
                    sp.wait_ge(free, first + j)
                    sp.dma_start(ring[:, (b + j) % RING, :], stream[b + j]).then_inc(loaded[(b + j) % RING], 16)
                b = end
            for b in range(TB):
                sp.wait_ge(of("result"), b + 1)
                sp.dma_start(out[b * P:(b + 1) * P, :], arena[:, b * D:(b + 1) * D]).then_inc(out_done, 16)
            sp.wait_ge(out_done, 16 * TB)

        @block.tensor
        def _(pe):
            ident = col("ident")
            pe.wait_ge(cols_loaded, 16)

            def transposes_of_x(v, all_of_hT=True):
                for k in range(KD):
                    if k < 1:
                        pe.wait_ge(xn_ready, TB * (v + 1 - (v >= NORM_OF["swa"])))
                    for b in range(TB):
                        last = pe.transpose(ps[:, k // 2, (k % 2) * T + b * P:(k % 2) * T + (b + 1) * P],
                                            xn[:, b, k * P:(k + 1) * P], ident)
                    if k % 2:
                        last.then_inc(xT_ready, 1)
                if all_of_hT:
                    pe.wait_ge(hT_d, hT_by[v + 1])

            def by_row_blocks(first, n, lhsT, banks=0):
                for k in range(n):
                    wait_loaded(pe, first + k)
                    for b in range(TB):
                        for half in range(2):
                            last = pe.matmul(ps[:, banks + 2 * b + half, :], lhsT(k, b),
                                             ring[:, (first + k) % RING, half * 512:half * 512 + 512],
                                             start=k == 0, stop=k == n - 1)
                    last.then_inc(used, 1)

            def products(dst, a, b, start, stop):
                pe.matmul(dst, a[0], b[0], start=start, stop=False)
                pe.matmul(dst, a[0], b[1], start=False, stop=False)
                return pe.matmul(dst, a[1], b[0], start=False, stop=stop)

            def split_column_block(b, dst, i=None, per_turn=0, hT_before=None):
                wait_split(pe, b, i, per_turn)
                for k in range(KD):
                    if hT_before is not None:
                        pe.wait_ge(hT_d, hT_before + k + 1)
                    c = slice(k * P, (k + 1) * P)
                    last = products(dst, (ring_hi[:, b % SLOTS, c], ring_lo[:, b % SLOTS, c]),
                                    (hT_hi[:, k, :], hT_lo[:, k, :]), k == 0, k == KD - 1)
                last.then_inc(used, 1)

            def h_tiles(k, b):
                t = slice(b * P, (b + 1) * P)
                return hT_hi[:, k, t], hT_lo[:, k, t]

            def ring_parts(b, c):
                return ring_hi[:, b % SLOTS, c], ring_lo[:, b % SLOTS, c]

            def split_row_blocks(first, n, banks=0):
                for k in range(n):
                    wait_split(pe, first + k)
                    for b in range(TB):
                        for half in range(2):
                            last = products(ps[:, banks + 2 * b + half, :], h_tiles(k, b),
                                            ring_parts(first + k, slice(half * 512, half * 512 + 512)),
                                            k == 0, k == n - 1)
                    last.then_inc(used, 1)

            def split_down(b, slot, i=None, per_turn=0, start=False, stop=False):
                wait_split(pe, b, i, per_turn)
                for tb in range(TB):
                    t = slice(tb * P, (tb + 1) * P)
                    for half in range(2):
                        c = slice(half * 512, half * 512 + 512)
                        last = products(ps[:, 2 * tb + half, :], (w_hi[:, slot, t], w_lo[:, slot, t]),
                                        (ring_hi[:, b % SLOTS, c], ring_lo[:, b % SLOTS, c]), start, stop)
                last.then_inc(used, 1)

            def ffn(f, name):
                transposes_of_x(NORM_OF[name], all_of_hT=False)
                base, done = AT[name], FC * f

                def up(c, b, i=None):
                    split_column_block(b, ps[:, 4 + c % 2, 0:T], i, 12, hT_by[NORM_OF[name]] if c == 0 else None)
                    split_column_block(b + 1, ps[:, 4 + c % 2, T:2 * T], i, 12)

                def down(c, b, i=None, start=False, stop=False):
                    split_down(b, c % 2, i, 12, start, stop)

                up(0, base)
                up(1, base + 2)
                pe.wait_ge(hidden_ready, done + 1)
                down(0, base + 4, start=True)
                with pe.Fori(0, 5) as i:
                    for j in range(4):
                        c = 1 + j
                        pe.wait_ge(hidden_ready, i * 4 + (done + c))
                        up(c + 1, base + 2 + 3 * c, i)
                        pe.wait_ge(hidden_ready, i * 4 + (done + c + 1))
                        down(c, base + 4 + 3 * c, i)
                pe.wait_ge(hidden_ready, done + FC)
                down(1, base + 3 * FC - 1, stop=True)

            def stick_breaking():
                transposes_of_x(NORM_OF["sb"])
                base = AT["sb_qkv"]
                R = sb_regions()
                pairs = HEADS // 2

                def project(j, part):
                    b = base + 3 * j
                    if part == 0:
                        if j >= 2:
                            pe.wait_ge(of("sb_qk"), j - 1)
                        split_column_block(b, ps[:, j % 2, 0:T])
                        split_column_block(b + 1, ps[:, j % 2, T:2 * T])
                        return
                    if j >= 2:
                        pe.wait_ge(of("sb_v"), j - 1)
                    wait_split(pe, b + 2)
                    for tb in range(TB):
                        for k in range(KD):
                            last = products(ps[:, 2 + j % 2, tb * P:(tb + 1) * P], h_tiles(k, tb),
                                            ring_parts(b + 2, slice(k * P, (k + 1) * P)), k == 0, k == KD - 1)
                    last.then_inc(used, 1)

                project(0, 0)
                project(0, 1)
                for j in range(pairs):
                    q, k_, v_ = R["q"][:, j % 2], R["k"][:, j % 2], R["v"][:, j % 2]
                    pe.wait_ge(of("sb_qk"), j + 1)
                    if j >= 1:
                        pe.wait_ge(of("sb_o"), j)
                    for e in range(2):
                        h = slice(64 * e, 64 * e + 64)
                        pe.matmul(ps[:, 4 + e, 0:T], k_[h, 0:P], q[h, :], start=True, stop=True)
                        last = pe.matmul(ps[:, 4 + e, T:T + P], k_[h, P:T], q[h, P:T], start=True, stop=True)
                    last.then_inc(of("sb_s"), 1)
                    if j + 1 < pairs:
                        project(j + 1, 0)
                    pe.wait_ge(of("sb_sp"), j + 1)
                    if j >= 1:
                        pe.wait_ge(of("sb_t"), j)
                    for e in range(2):
                        sp_ = R["sp"][:, e]
                        pe.matmul(ps[:, 6 + e, 0:T], col("lo_incl"), sp_[:, 0:T], start=True, stop=False)
                        pe.matmul(ps[:, 6 + e, P:T], col("ones"), sp_[:, T:T + P], start=False, stop=True)
                        last = pe.matmul(ps[:, 6 + e, T:T + P], col("lo_incl"), sp_[:, T:T + P],
                                         start=True, stop=True)
                    last.then_inc(of("sb_r"), 1)
                    if j + 1 < pairs:
                        project(j + 1, 1)
                    pe.wait_ge(of("sb_a"), j + 1)
                    pe.wait_ge(of("sb_v"), j + 1)
                    for e in range(2):
                        o = ps[64 * e:64 * e + 64, 4, 0:T]
                        a_ = R["a"][:, e]
                        pe.matmul(o, v_[:, 0, 64 * e:64 * e + 64], a_[:, 0:T], start=True, stop=False)
                        last = pe.matmul(ps[64 * e:64 * e + 64, 4, P:T], v_[:, 1, 64 * e:64 * e + 64],
                                         a_[:, T:T + P], start=False, stop=True)
                    last.then_inc(of("sb_av"), 1)
                pe.wait_ge(of("sb_o"), pairs)
                by_row_blocks(AT["sb_out"], KD, lambda k, b: R["oT"][:, k, b * P:(b + 1) * P])

            def attention(a, R):
                pairs, n0 = HEADS // 2, a * (HEADS // 2)

                def turn_q(j):
                    if j >= 1:
                        pe.wait_ge(of("att_qk"), n0 + j)
                    if a == 0:
                        for e in range(2):
                            for part in range(2):
                                src = R["qk"[part]]
                                for tb in range(TB):
                                    h = (2 * j + e) * QD
                                    o = part * T + tb * P
                                    last = pe.transpose(ps[0:QD, e, o:o + P], src[:, tb, h:h + QD], ident)
                    else:
                        for tb in range(TB):
                            last = pe.transpose(ps[:, 0, tb * P:(tb + 1) * P],
                                                R["q"][:, tb, j * P:(j + 1) * P], ident)
                    last.then_inc(of("att_t"), 1)

                def scores(j):
                    pe.wait_ge(of("att_qk"), n0 + j + 1)
                    if j >= 1:
                        pe.wait_ge(of("att_m"), n0 + j)
                    for e in range(2):
                        if a == 0:
                            qT, kT = R["qkT"][0:QD, j % 2, e, 0:T], R["qkT"][0:QD, j % 2, e, T:2 * T]
                        else:
                            h = slice(64 * e, 64 * e + 64)
                            qT, kT = R["qT"][h, j % 2, :], R["kT"][h, 2 * j // 8, :]
                        pe.matmul(ps[:, 2 + e, 0:P], qT[:, 0:P], kT[:, 0:P], start=True, stop=True)
                        last = pe.matmul(ps[:, 2 + e, P:3 * P], qT[:, P:T], kT, start=True, stop=True)
                    last.then_inc(of("att_s"), 1)

                def turn_p(j):
                    pe.wait_ge(of("att_n"), n0 + j + 1)
                    if j >= 1:
                        pe.wait_ge(of("att_w"), n0 + j)
                    for e in range(2):
                        for s in range(3):
                            last = pe.transpose(ps[:, 4 + e, s * P:(s + 1) * P],
                                                R["p"][:, j % 2, e, s * P:(s + 1) * P], ident)
                    last.then_inc(of("att_pT"), 1)

                def values(j):
                    pe.wait_ge(of("att_w"), n0 + j + 1)
                    if j >= 2:
                        pe.wait_ge(of("att_o"), n0 + j - 1)
                    for e in range(2):
                        h = slice(64 * e, 64 * e + 64)
                        for kb in range(TB):
                            if a == 0:
                                v = R["v"][:, kb, (2 * j + e) * 64:(2 * j + e) * 64 + 64]
                            else:
                                o = P + (2 * j // 8) * 64
                                v = R["kv"][:, kb, o:o + 64]
                            last = pe.matmul(ps[h, 6 + j % 2, kb * P:T], v, R["pT"][:, e, kb * T:T + kb * P],
                                             start=kb == 0, stop=kb == 1)
                    last.then_inc(of("att_av"), 1)

                turn_q(0)
                scores(0)
                turn_q(1)
                for j in range(pairs):
                    if j + 1 < pairs:
                        scores(j + 1)
                    turn_p(j)
                    if j + 2 < pairs:
                        turn_q(j + 2)
                    values(j)
                pe.wait_ge(of("att_o"), n0 + pairs)
                by_row_blocks(AT["mla_out"] if a == 0 else AT["swa_out"], KD,
                              lambda k, b: R["oT"][:, k, b * P:(b + 1) * P])

            def mla():
                transposes_of_x(NORM_OF["mla"])
                R = attention_regions(0)
                base = AT["mla_in"]
                for k in range(KD):
                    b = base + k // 2
                    if k % 2 == 0:
                        wait_split(pe, b)
                    for tb in range(TB):
                        last = products(ps[:, tb, 0:MLA_IN], h_tiles(k, tb),
                                        ring_parts(b, slice((k % 2) * MLA_IN, (k % 2 + 1) * MLA_IN)),
                                        k == 0, k == KD - 1)
                    if k % 2:
                        last.then_inc(used, 1)
                pe.wait_ge(of("mla_cn"), 1)
                for c in range(3):
                    for tb in range(TB):
                        last = pe.transpose(ps[:, 2 + c // 2, (c % 2) * T + tb * P:(c % 2) * T + (tb + 1) * P],
                                            R["cn"][:, tb, c * P:(c + 1) * P], ident)
                last.then_inc(of("mla_cT"), 1)
                pe.wait_ge(of("mla_cTs"), 1)
                for n in range(3):
                    b = AT["mla_uq"] + n
                    wait_loaded(pe, b)
                    for tb in range(TB):
                        for k in range(2):
                            last = pe.matmul(ps[:, 4 * tb + n, :], R["cT"][:, k, tb * P:(tb + 1) * P],
                                             ring[:, b % RING, k * 512:(k + 1) * 512], start=k == 0, stop=k == 1)
                    last.then_inc(used, 1)
                pe.wait_ge(of("mla_q"), 1)
                for n in range(2):
                    b = AT["mla_ukv"] + n
                    wait_loaded(pe, b)
                    for tb in range(TB):
                        for half in range(2):
                            last = pe.matmul(ps[:, 4 * tb + 2 * n + half, :], R["cT"][:, 2, tb * P:(tb + 1) * P],
                                             ring[:, b % RING, half * 512:(half + 1) * 512], start=True, stop=True)
                    last.then_inc(used, 1)
                pe.wait_ge(of("mla_kv_a"), 1)
                pe.wait_ge(of("mla_kv_d"), 1)
                attention(0, R)

            def swa():
                R = attention_regions(1)
                transposes_of_x(NORM_OF["kv"])
                for k in range(KD):
                    b = AT["swa_kv"] + k // 4
                    if k % 4 == 0:
                        wait_split(pe, b)
                    for tb in range(TB):
                        last = products(ps[:, 4 + tb, 0:256], h_tiles(k, tb),
                                        ring_parts(b, slice((k % 4) * 256, (k % 4 + 1) * 256)),
                                        k == 0, k == KD - 1)
                    if k % 4 == 3:
                        last.then_inc(used, 1)
                transposes_of_x(NORM_OF["swa"])
                split_row_blocks(AT["swa_q"], KD)
                pe.wait_ge(of("swa_k"), 1)
                for g in range(2):
                    for tb in range(TB):
                        last = pe.transpose(ps[:, 6, g * T + tb * P:g * T + (tb + 1) * P], R["kd"][:, tb, g, :], ident)
                last.then_inc(of("swa_kT"), 1)
                pe.wait_ge(of("swa_q"), 1)
                pe.wait_ge(of("swa_kTs"), 1)
                attention(1, R)

            def ssm():
                R = ssm_regions()
                transposes_of_x(NORM_OF["ssm"])
                for half in range(2):
                    split_row_blocks(AT["ssm_z"] + 8 * half, KD, banks=4 * half)
                base = AT["ssm_xbc"]
                pe.wait_ge(of("ssm_z"), 1)
                for c in range(4):
                    split_column_block(base + c, ps[:, c, 0:T])
                with pe.Fori(0, CONV_TILES // 4 - 1) as i:
                    for j in range(4):
                        pe.wait_ge(of("conv_taps"), i * 12 + (3 * j + 3))
                        split_column_block(base + 4 + j, ps[:, j, 0:T], i, 4)
                pe.wait_ge(of("ssm_z"), 2)
                b = AT["ssm_dt"]
                wait_split(pe, b)
                for tb in range(TB):
                    for k in range(KD):
                        last = products(ps[:, 4, tb * SH:(tb + 1) * SH], h_tiles(k, tb),
                                        ring_parts(b, slice(k * SH, (k + 1) * SH)), k == 0, k == KD - 1)
                last.then_inc(used, 1)
                pe.wait_ge(of("ssm_a"), 1)
                pe.matmul(ps[:, 5, 0:64], col("up_incl"), R["a"], start=True, stop=True)
                pe.matmul(ps[:, 5, 64:128], col("ones"), R["a"], start=True, stop=True).then_inc(of("ssm_cs"), 1)
                pe.wait_ge(of("conv_done"), CONV_TILES)
                for n in range(8):
                    if n >= 4:
                        pe.wait_ge(of("ssm_xs"), n - 3)
                    for q in range(4):
                        last = pe.transpose(ps[:, n % 4, q * P:(q + 1) * P],
                                            R["xc"][:, 4 * (n // 2) + q, (n % 2) * P:(n % 2 + 1) * P], ident)
                    last.then_inc(of("ssm_xT"), 1)
                for n in range(2):
                    for q in range(4):
                        last = pe.transpose(ps[:, 6 + n, q * P:(q + 1) * P], R["xc"][:, 16 + 4 * n + q, 0:P], ident)
                    last.then_inc(of("ssm_xT"), 1)
                pe.wait_ge(of("ssm_xs"), 10)

                def sums(n):
                    g, c = n // 2, n % 2
                    pe.wait_ge(of("sg_ta"), n + 1)
                    if n >= 2:
                        pe.wait_ge(of("sg_seg"), n - 1)
                        pe.wait_ge(of("sg_M"), n - 1)
                    pe.matmul(ps[:, n % 2, :], col("ones"), R["ta"][:, n % 2].rearrange("p a b -> p (a b)"),
                              start=True, stop=True)
                    pe.matmul(ps[:, 2 + n % 2, 0:P], R["xc"][:, 16 + g, c * P:(c + 1) * P],
                              R["xc"][:, 24 + g, c * P:(c + 1) * P], start=True, stop=True).then_inc(of("sg_cb"), 1)

                sums(0)
                for n in range(2 * SG):
                    g, c = n // 2, n % 2
                    if n + 1 < 2 * SG:
                        sums(n + 1)
                    pe.wait_ge(of("sg_M"), n + 1)
                    if n >= 2:
                        pe.wait_ge(of("sg_o"), n - 1)
                    if c == 0 and g >= 2:
                        pe.wait_ge(of("sg_st"), g - 1)
                    if c == 1:
                        pe.wait_ge(of("sg_st"), g + 1)
                    for q in range(HPG):
                        o = (HPG * g + q) * 64
                        last = pe.matmul(ps[:, 4 + n % 2, q * 64:(q + 1) * 64], R["M"][:, n % 2, q, :],
                                         R["X"][:, c, o:o + 64], start=True, stop=True)
                    if c == 0:
                        last = pe.matmul(ps[:, 6 + g % 2, 0:T], R["Bl"][:, g, :], R["Xd"][:, g % 2, :],
                                         start=True, stop=True)
                    else:
                        last = pe.matmul(ps[:, 4 + n % 2, T:2 * T], R["xc"][:, 24 + g, P:T], R["st"][:, g % 2, :],
                                         start=True, stop=True)
                    last.then_inc(of("sg_y"), 1)
                pe.wait_ge(of("ssm_yn"), TB)
                for k in range(DI // P):
                    for tb in range(TB):
                        last = pe.transpose(ps[:, k // 2, (k % 2) * T + tb * P:(k % 2) * T + (tb + 1) * P],
                                            R["zs"][:, tb, k * P:(k + 1) * P], ident)
                    if k % 2:
                        last.then_inc(of("ssm_yT"), 1)
                pe.wait_ge(of("ssm_yT_a"), 8)
                pe.wait_ge(of("ssm_yT_d"), 8)
                by_row_blocks(AT["ssm_out"], DI // P, lambda k, b: R["yT"][:, k, b * P:(b + 1) * P])

            def peer(l):
                R = peer_regions()
                transposes_of_x(NORM_OF[f"peer{l}"])
                base, n0 = AT[f"peer{l}_q"], SUBS * l
                subkeys = col("subkeys", 2, 2, KEYS)

                def key_scores(m):
                    pe.wait_ge(of("peer_qT"), n0 + m + 1)
                    if m >= 2:
                        pe.wait_ge(of("peer_s"), n0 + m - 1)
                    for tb in range(TB):
                        last = pe.matmul(ps[:, 2 + m % 2, tb * P:(tb + 1) * P],
                                         R["qT"][:, m % 2, tb * P:(tb + 1) * P], subkeys[:, l, m % 2, :],
                                         start=True, stop=True)
                    last.then_inc(of("peer_sp"), 1)

                for m in range(SUBS):
                    if m >= 2:
                        pe.wait_ge(of("peer_qT"), n0 + m - 1)
                    split_column_block(base + m, ps[:, m % 2, 0:T])
                    if m >= 1:
                        key_scores(m - 1)
                key_scores(SUBS - 1)
                base, n0 = AT[f"peer{l}_u"], 64 * l
                for n in range(4):
                    for j in range(2):
                        split_column_block(base + 2 * n + j, ps[:, 4 + n, j * T:(j + 1) * T])
                with pe.Fori(0, KEYS // 8 - 1) as i:
                    for n in range(4):
                        pe.wait_ge(of("gelu"), i * 4 + (n0 + n + 1))
                        for j in range(2):
                            split_column_block(base + 8 + 2 * n + j, ps[:, 4 + n, j * T:(j + 1) * T], i, 8)
                pe.wait_ge(of("picks"), l + 1)
                for c in range(3):
                    for tb in range(TB):
                        last = pe.transpose(ps[:, c // 2, (c % 2) * T + tb * P:(c % 2) * T + (tb + 1) * P],
                                            R["pk"][:, c, tb, :], ident)
                last.then_inc(of("picksT"), 1)
                pe.wait_ge(of("picksTs"), l + 1)

                def gates(n):
                    for q in range(4):
                        last = pe.matmul(ps[:, n, q * P:(q + 1) * P], R["hot"][:, n % 2, 0, q, :],
                                         R["hot"][:, n % 2, 1, q, :], start=True, stop=True)
                    last.then_inc(of("gates"), 1)

                def wait_hot(n, i=None):
                    for name in ("hot", "hot_by_act"):
                        pe.wait_ge(of(name), count(n0 + n + 1, i, 4))

                for n in range(4):
                    wait_hot(n)
                    gates(n)
                with pe.Fori(0, 15) as i:
                    for n in range(4):
                        wait_hot(n + 4, i)
                        pe.wait_ge(of("gated"), i * 4 + (n0 + n + 1))
                        gates(n)
                pe.wait_ge(of("gated"), n0 + 64)
                base, n0 = AT[f"peer{l}_v"], KEYS * l

                def down(j, i=None, start=False, stop=False):
                    pe.wait_ge(of("peer_w"), count(n0 + j + 1, i, 4))
                    split_down(base + j, j % 2, i, 4, start, stop)

                for j in range(4):
                    down(j, start=j == 0)
                with pe.Fori(0, KEYS // 4 - 2) as i:
                    for j in range(4, 8):
                        down(j, i)
                for j in range(KEYS - 4, KEYS):
                    down(j, stop=j == KEYS - 1)

            def ple(l):
                transposes_of_x(NORM_OF[f"ple{l}"])
                split_row_blocks(AT[f"ple{l}_gate"], KD)
                pT = split(own_columns(f"ple{l}"), 2, T)
                pe.wait_ge(own_loaded, 16 * (own_before(f"ple{l}") + 1))
                by_row_blocks(AT[f"ple{l}_proj"], 2, lambda k, b: pT[:, k, b * P:(b + 1) * P], banks=4)


            fs = 0
            for name in LAYERS:
                if name.startswith("ffn"):
                    ffn(fs, name)
                    fs += 1
                elif name == "sb":
                    stick_breaking()
                elif name in ("mla", "swa", "ssm"):
                    {"mla": mla, "swa": swa, "ssm": ssm}[name]()
                elif name.startswith("peer"):
                    peer(int(name[-1]))
                elif name.startswith("ple"):
                    ple(int(name[-1]))

        @block.scalar
        def _(act):
            link = link_for(act, act_chain)
            firsts = [0]

            def load_row(n, slot):
                act.dma_start(row[:, slot, :], rows_in[n:n + 1, :].rearrange("a n -> (a n)")
                              .partition_broadcast(P)).then_inc(row_loaded[slot], 16)

            def squares(parts, into=arena):
                at = 0
                for n, (src, w) in enumerate(parts):
                    junk = into[:, at:at + w]
                    at += w
                    last = act.activation(junk, src, ACT.Square, accum_out=ss[:, n:n + 1])
                last.then_inc(ss_ready, 1)

            def squares_of_x(updates):
                if not updates:
                    act.wait_ge(x_loaded, 16)
                for b in range(TB):
                    if updates:
                        act.wait_ge((x_first, x_ready)[b], updates)
                    last = act.activation(arena[:, b * D:(b + 1) * D], x[:, b, :], ACT.Square, accum_out=ss[:, b:b + 1])
                last.then_inc(ss_ready, 1)

            def norm_in(name):
                v = NORM_OF[name]
                if name in FIRST_PART:
                    for b in range(SLOTS):
                        make_hi(act, AT[FIRST_PART[name]] + b)
                if name != "swa":
                    squares_of_x(x_of[name])
                if name in OWN_OF and name != "swa" or name == "kv":
                    own, w = OWN_OF["swa" if name == "kv" else name]
                    act.dma_start(own_columns("swa" if name == "kv" else name),
                                  cols_in[:, CAT[own][0]:CAT[own][0] + w]).then_inc(own_loaded, 16)
                for k in range(KD):
                    if k % 2 == 0:
                        act.wait_ge(xT_ready, 4 * v + k // 2 + 1)
                    act.activation(hT_hi[:, k, :], ps[:, k // 2, (k % 2) * T:(k % 2 + 1) * T], ACT.Copy,
                                   scale=gain(v, k)).then_inc(hT_a, 1)

            def squares_of_banks():
                for b, done in enumerate((first_squared, ss_ready)):
                    act.activation(arena[:, KEYS * T - D:KEYS * T], bank(2 * b, 2), ACT.Square,
                                   accum_out=ss[:, b:b + 1]).then_inc(done, 1)
                    if b == 0:
                        firsts[0] += 1
                        act.wait_ge(first_squared, firsts[0])

            def ffn(f, name):
                norm_in(name)
                load_row(f if f == 0 else {1: 2, 2: 3, 3: 5}[f], 0)
                base, done = AT[name], FC * f
                hid = region(ARENA, 2, 2, T)[0]

                def silu(c):
                    return act.activation(hid[:, 0, c % 2, :], ps[:, 4 + c % 2, 0:T], ACT.Silu)

                act.wait_ge(used, base + 2)
                silu(0).then_inc(silu_ready, 1)
                make_hi(act, base + 4)
                make_hi(act, base + 5)
                act.wait_ge(used, base + 4)
                silu(1).then_inc(silu_ready, 1)
                with act.Fori(0, 5) as i:
                    for j in range(4):
                        c = 2 + j
                        for b in range(3 * c, 3 * c + 3):
                            make_hi(act, base + b, i, 12)
                        act.wait_ge(used, i * 12 + (base + 3 * c + 1))
                        act.wait_ge(hidden_ready, i * 4 + (done + c - 1))
                        silu(c).then_inc(silu_ready, 1)
                act.wait_ge(used, base + 3 * FC)
                squares_of_banks()

            def stick_breaking():
                norm_in("sb")
                load_row(1, 0)
                base = AT["sb_qkv"]
                R = sb_regions()
                pairs = HEADS // 2

                def evac(j):
                    if j >= 2:
                        act.wait_ge(of("sb_av"), j - 1)
                    act.wait_ge(used, base + 3 * j + 2)
                    act.activation(R["q"][:, j % 2], ps[:, j % 2, 0:T], ACT.Copy, scale=0.125)
                    act.activation(R["k"][:, j % 2], ps[:, j % 2, T:2 * T], ACT.Copy).then_inc(of("sb_qk"), 1)

                def ahead(*blocks):
                    for b in blocks:
                        if b < 3 * pairs:
                            make_hi(act, base + b)

                evac(0)
                ahead(4, 5)
                for j in range(pairs):
                    act.wait_ge(of("sb_s"), j + 1)
                    act.wait_ge(of("sb_sp"), j) if j else None
                    link(act.activation(R["az"][:, :, :], ps[:, 4:6, 0:384], ACT.Abs))
                    link(act.activation(R["ez"][:, :, :], R["az"][:, :, :], ACT.Exp, scale=-1.0))
                    act.activation(R["lz"][:, :, :], R["ez"][:, :, :], ACT.Ln, bias=1.0).then_inc(of("sb_l"), 1)
                    ahead(3 * j + 6)
                    if j + 1 < pairs:
                        evac(j + 1)
                    ahead(3 * j + 7)
                    act.wait_ge(of("sb_t"), j + 1)
                    act.wait_ge(of("sb_av"), j) if j else None
                    act.activation(R["a"][:, :, :], R["t"][:, :, :], ACT.Exp).then_inc(of("sb_a"), 1)
                    ahead(3 * j + 8)
                act.wait_ge(used, AT["sb_out"] + KD)
                squares_of_banks()

            def attention(a, R):
                pairs, n0 = HEADS // 2, a * (HEADS // 2)

                def take_q(j):
                    act.wait_ge(of("att_t"), n0 + j + 1)
                    if j >= 2:
                        act.wait_ge(of("att_s"), n0 + j - 1)
                    if a == 0:
                        act.activation(R["qkT"][0:QD, j % 2], ps[0:QD, 0:2, :], ACT.Copy).then_inc(of("att_qk"), 1)
                    else:
                        act.activation(R["qT"][:, j % 2], ps[:, 0, 0:T], ACT.Copy).then_inc(of("att_qk"), 1)

                def exps(j):
                    act.wait_ge(of("att_m"), n0 + j + 1)
                    if j >= 2:
                        act.wait_ge(of("att_pT"), n0 + j - 1)
                    for e in range(2):
                        for tb in range(TB):
                            c = slice(0, P) if tb == 0 else slice(P, 3 * P)
                            k = 2 * e + tb
                            last = act.activation(R["p"][:, j % 2, e, c], R["st"][:, j % 2, e, c], ACT.Exp,
                                                  bias=R["nm"][:, j % 2, k:k + 1],
                                                  accum_out=R["su"][:, j % 2, k:k + 1])
                        if a:
                            last = act.activation(R["es"][:, j % 2, 2 * e:2 * e + 2],
                                                  R["nm"][:, j % 2, 2 * e:2 * e + 2], ACT.Exp,
                                                  bias=col("sinks")[:, 2 * j + e:2 * j + e + 1])
                    last.then_inc(of("att_p"), 1)

                def take_p(j):
                    act.wait_ge(of("att_pT"), n0 + j + 1)
                    if j >= 1:
                        act.wait_ge(of("att_av"), n0 + j)
                    act.activation(R["pT"][:, :, :], ps[:, 4:6, 0:384], ACT.Copy).then_inc(of("att_w"), 1)

                take_q(0)
                take_q(1)
                exps(0)
                for j in range(pairs):
                    if j + 1 < pairs:
                        exps(j + 1)
                    take_p(j)
                    if j + 2 < pairs:
                        take_q(j + 2)

            def mla():
                norm_in("mla")
                load_row(4, 0)
                R = attention_regions(0)
                act.wait_ge(used, AT["mla_in"] + 4)
                for tb in range(TB):
                    last = act.activation(R["mp"][:, tb, :], ps[:, tb, 0:MLA_IN], ACT.Copy)
                link(last)
                squares([(R["mp"][:, tb, 0:QL], QL) for tb in range(TB)] +
                        [(R["mp"][:, tb, QL:QL + KVL], KVL) for tb in range(TB)])
                act.wait_ge(of("mla_cT"), 1)
                for c in range(3):
                    g = col("q_norm")[:, c:c + 1] if c < 2 else col("kv_norm")
                    last = act.activation(R["cT"][:, c, :], ps[:, 2 + c // 2, (c % 2) * T:(c % 2 + 1) * T],
                                          ACT.Copy, scale=g)
                last.then_inc(of("mla_cTs"), 1)
                act.wait_ge(used, AT["mla_uq"] + 3)
                for tb in range(TB):
                    last = act.activation(R["q"][:, tb, :], bank(4 * tb, 3), ACT.Copy)
                last.then_inc(of("mla_q"), 1)
                act.wait_ge(used, AT["mla_ukv"] + 2)
                kv = bank(0, 4).rearrange("p (h c) -> p h c", h=HEADS)
                act.activation(split(R["k"][:, 0, :], HEADS, QD)[:, :, 0:64], kv[:, :, 0:64], ACT.Copy)
                act.activation(split(R["v"][:, 0, :], HEADS, 64), kv[:, :, 64:128], ACT.Copy)\
                   .then_inc(of("mla_kv_a"), 1)
                attention(0, R)
                act.wait_ge(used, AT["mla_out"] + KD)
                squares_of_banks()

            def swa():
                R = attention_regions(1)
                norm_in("kv")
                load_row(6, 0)
                load_row(8, 1)
                norm_in("swa")
                for b in range(2, KD):
                    make_hi(act, AT["swa_q"] + b)
                act.wait_ge(of("swa_kT"), 1)
                act.activation(R["kT"][:, :, :], ps[:, 6, :].rearrange("p (g t) -> p g t", g=2), ACT.Copy)\
                   .then_inc(of("swa_kTs"), 1)
                attention(1, R)

            def ssm():
                R = ssm_regions()
                norm_in("ssm")
                for half in range(2):
                    for b in (range(SLOTS, 11), range(11, 19))[half]:
                        make_hi(act, AT["ssm_z"] + b)
                    act.wait_ge(used, AT["ssm_z"] + 8 * half + 8)
                    for b in range(TB):
                        last = act.activation(R["zs"][:, b, half * D:(half + 1) * D], bank(4 * half + 2 * b, 2),
                                              ACT.Silu)
                    last.then_inc(of("ssm_z"), 1)
                base = AT["ssm_xbc"]
                conv = CAT["conv"][0]

                def silu(j, i=None):
                    act.wait_ge(of("conv_taps"), count(3 * j + 3, i, 12))
                    act.activation(R["xc"][:, bass.ds(count(j, i, 4), 1), :].rearrange("p a t -> p (a t)"),
                                   R["acc"][:, j % 4, :], ACT.Silu).then_inc(of("conv_done"), 1)

                def convolved(js, i=None):
                    for j in js:
                        if j < CONV_TILES - 2:
                            make_hi(act, base + j + 3, i, 4)
                        act.wait_ge(used, count(base + j + 1, i, 4))
                        if j >= 4:
                            act.wait_ge(of("conv_done"), count(j - 3, i, 4))
                        o = count(conv + 5 * j, i, 20)
                        act.activation(R["acc"][:, j % 4, :], ps[:, j % 4, 0:T], ACT.Identity,
                                       scale=cols[:, bass.ds(o + 3, 1)], bias=cols[:, bass.ds(o + 4, 1)])\
                           .then_inc(of("conv_acc"), 1)
                        if j >= 1:
                            silu(j - 1, i)

                convolved(range(4))
                with act.Fori(0, CONV_TILES // 4 - 2) as i:
                    convolved(range(4, 8), i)
                convolved(range(CONV_TILES - 4, CONV_TILES))
                silu(CONV_TILES - 1)
                act.wait_ge(of("ssm_u"), 1)
                act.activation(R["eA"], col("a_log"), ACT.Exp)
                link(act.activation(R["az"], R["u"], ACT.Abs))
                link(act.activation(R["ez"], R["az"], ACT.Exp, scale=-1.0))
                act.activation(R["lz"], R["ez"], ACT.Ln, bias=1.0).then_inc(of("ssm_l"), 1)
                act.wait_ge(of("ssm_de"), 1)
                act.activation(R["dte"], R["de"], ACT.Exp)
                act.activation(R["eacs"], R["acs"], ACT.Exp).then_inc(of("ssm_ex"), 1)
                for n in range(8):
                    act.wait_ge(of("ssm_xT"), n + 1)
                    act.activation(R["xs"][:, n % 2, (n // 2) * 512:(n // 2 + 1) * 512], ps[:, n % 4, :], ACT.Copy)\
                       .then_inc(of("ssm_xs"), 1)
                for n in range(2):
                    act.wait_ge(of("ssm_xT"), 9 + n)
                    act.activation(R["Bl"][:, 4 * n:4 * n + 4, :].rearrange("p a b -> p (a b)"), ps[:, 6 + n, :],
                                   ACT.Copy).then_inc(of("ssm_xs"), 1)

                def state(g):
                    act.wait_ge(of("sg_y"), 2 * g + 1)
                    act.activation(R["st"][:, g % 2, :], ps[:, 6 + g % 2, 0:T], ACT.Copy).then_inc(of("sg_st"), 1)

                for n in range(2 * SG):
                    act.wait_ge(of("sg_seg"), n + 1)
                    if n >= 2:
                        act.wait_ge(of("sg_M"), n - 1)
                    act.activation(R["L"][:, n % 2], R["seg"][:, n % 2], ACT.Exp).then_inc(of("sg_L"), 1)
                    if n % 2:
                        state(n // 2)
                act.wait_ge(of("sg_done"), 2 * SG)
                squares([(R["zs"][:, tb, g * T:(g + 1) * T], T) for tb in range(TB) for g in range(SG)],
                        R["X"][:, :, :].rearrange("p a b -> p (a b)"))
                for k in (0, 1, 4, 5, 8, 9, 12, 13):
                    act.wait_ge(of("ssm_yT"), k // 2 + 1)
                    act.activation(R["yT"][:, k, :], ps[:, k // 2, (k % 2) * T:(k % 2 + 1) * T], ACT.Copy,
                                   scale=col("gate_norm")[:, k:k + 1]).then_inc(of("ssm_yT_a"), 1)

            def peer(l):
                R = peer_regions()
                norm_in(f"peer{l}")
                base, n0 = AT[f"peer{l}_q"], SUBS * l
                for m in range(SUBS):
                    if m >= 1:
                        make_hi(act, base + m + SLOTS - 1)
                    act.wait_ge(used, base + m + 1)
                    if m >= 2:
                        act.wait_ge(of("peer_sp"), n0 + m - 1)
                    act.activation(R["qT"][:, m % 2, :], ps[:, m % 2, 0:T], ACT.Copy).then_inc(of("peer_qT"), 1)
                base, n0 = AT[f"peer{l}_u"], 64 * l

                def gelus(first, turns):
                    with act.Fori(0, turns) as i:
                        for n in range(4):
                            for b in range(2):
                                make_hi(act, base + first + 2 * n + 3 + b, i, 8)
                            act.wait_ge(used, i * 8 + (base + first + 2 * n + 2))
                            act.activation(R["A"][:, bass.ds(i * 8 + (first + 2 * n), 2), :]
                                           .rearrange("p a t -> p (a t)"), ps[:, 4 + n, :], ACT.Gelu)\
                               .then_inc(of("gelu"), 1)

                gelus(0, LATE // 8)
                act.wait_ge(of("peer_e"), l + 1)
                act.activation(R["e"], R["e"], ACT.Exp).then_inc(of("peer_ex"), 1)
                act.wait_ge(of("picks"), l + 1)
                gelus(LATE, (KEYS - LATE) // 8)
                act.wait_ge(of("picksT"), l + 1)
                act.activation(pick[:, 0:2, :], ps[:, 0, :].rearrange("p (a t) -> p a t", a=2), ACT.Copy)
                act.activation(pick[:, 2, :], ps[:, 1, 0:T], ACT.Copy).then_inc(of("picksTs"), 1)
                base, n0 = AT[f"peer{l}_v"], KEYS * l
                make_hi(act, base + SLOTS - 1)
                n1 = 64 * l

                def hot(n, i=None):
                    t = count(4 * n, i, 16)
                    if n >= 2:
                        act.wait_ge(of("gates"), count(n1 + n - 1, i, 4))
                    for q in range(HOT_BY_DVE, 4):
                        last = act.activation(R["hot"][:, n % 2, 0, q], col("iota"), ACT.Abs, scale=-1.0,
                                              bias=pick[:, 0, bass.ds(t + q, 1)])
                    last.then_inc(of("distance"), 1)
                    act.wait_ge(of("distance"), count(n1 + n + 1, i, 4))
                    rows = R["hot"][:, n % 2, 0, HOT_BY_DVE:4]
                    act.activation(rows, rows, ACT.Relu, scale=-1.0, bias=1.0).then_inc(of("hot_by_act"), 1)

                act.wait_ge(of("picksTs"), l + 1)
                hot_loop(act, hot)
                act.wait_ge(of("gated"), 64 * l + 64)

                def take(j, i=None):
                    at = j if i is None else i * 4 + j
                    if j >= 2:
                        act.wait_ge(used, at + (base - 1))
                    act.activation(w_hi[:, j % 2, :], gated_tile(R, j, i), ACT.Copy).then_inc(of("peer_wh"), 1)

                def hi_and_take(js, i=None):
                    for j in js:
                        take(j, i)
                        if 2 <= j < KEYS - 2:
                            make_hi(act, base + j + 2, i, 4)

                hi_and_take(range(4))
                with act.Fori(0, KEYS // 4 - 2) as i:
                    hi_and_take(range(4, 8), i)
                hi_and_take(range(KEYS - 4, KEYS))

            def ple(l):
                norm_in(f"ple{l}")
                for b in range(SLOTS, KD):
                    make_hi(act, AT[f"ple{l}_gate"] + b)
                act.wait_ge(used, AT[f"ple{l}_gate"] + KD)
                sg = region(ARENA + 2 * T, TB, D)[0]
                for b in range(TB):
                    last = act.activation(sg[:, b, :], bank(2 * b, 2), ACT.Sigmoid)
                last.then_inc(of("ple_gate"), 1)


            act.wait_ge(cols_loaded, 16)
            act.wait_ge(of("angle"), 1)
            act.activation(ang[:, 2], ang[:, 1], ACT.Abs).then_inc(of("angle_abs"), 1)
            act.wait_ge(of("angle"), 2)
            act.activation(sinT[:, :, :], ang[:, 1], ACT.Sin)
            act.activation(cosT[:, :, :], ang[:, 3], ACT.Sin).then_inc(of("angle_sin"), 1)
            fs = 0
            for name in LAYERS:
                if name.startswith("ffn"):
                    ffn(fs, name)
                    fs += 1
                elif name == "sb":
                    stick_breaking()
                elif name in ("mla", "swa", "ssm"):
                    {"mla": mla, "swa": swa, "ssm": ssm}[name]()
                elif name.startswith("peer"):
                    peer(int(name[-1]))
                elif name.startswith("ple"):
                    ple(int(name[-1]))
            squares_of_x(len(LAYERS))
            load_row(7, 0)

        @block.vector
        def _(dve):
            link = link_for(dve, dve_chain)
            stats = [0]
            rows = [0, 0]

            def row_wait(slot):
                rows[slot] += 16
                dve.wait_ge(row_loaded[slot], rows[slot])

            firsts = [0]

            def rstd(parts):
                means(parts)
                dve.wait_ge(rs_ready, stats[0])

            def means(parts):
                stats[0] += 1
                dve.wait_ge(ss_ready, stats[0])
                for a, b, scale, eps in parts:
                    last = dve.tensor_scalar(ms[:, a:b], ss[:, a:b], scale, eps, ALU.mult, ALU.add)
                last.then_inc(ms_ready, 1)

            def own_wait(name):
                dve.wait_ge(own_loaded, 16 * (own_before(name) + 1))

            def norm_in(name):
                if name in POOL_BLOCKS:
                    stats_before[name] = stats[0]
                v = NORM_OF[name]
                if name.startswith("ffn"):
                    for b in range(2):
                        make_lo(dve, AT[name] + b)
                if name != "swa":
                    rstd([(0, TB, 1.0 / D, EPS)])
                    for b in range(TB):
                        dve.tensor_scalar(xn[:, b, :], x[:, b, :], rs[:, b:b + 1], None, ALU.mult)\
                           .then_inc(xn_ready, 1)
                for k in range(KD):
                    if k % 2 == 0:
                        dve.wait_ge(hT_a, hT_by[v] + k + 2)
                    dve.scalar_tensor_tensor(hT_lo[:, k, :], ps[:, k // 2, (k % 2) * T:(k % 2 + 1) * T],
                                             gain(v, k), hT_hi[:, k, :].bitcast(F32), ALU.mult, ALU.subtract)\
                       .then_inc(hT_d, 1)
                if name.startswith("ffn"):
                    for b in range(2, SLOTS):
                        make_lo(dve, AT[name] + b)

            def add_normed(weight):
                firsts[0] += 1
                row_wait(0)
                for b in range(TB):
                    if b == 0:
                        dve.wait_ge(first_squared, firsts[0])
                        dve.tensor_tensor(xn[:, b, :], bank(2 * b, 2), row[:, 0, :], ALU.mult)
                    else:
                        means([(0, TB, 1.0 / (D * weight * weight), EPS / (weight * weight))])
                        link(dve.tensor_tensor(xn[:, b, :], bank(2 * b, 2), row[:, 0, :], ALU.mult))
                dve.wait_ge(rs_ready, stats[0])
                for b in range(TB):
                    dve.scalar_tensor_tensor(x[:, b, :], xn[:, b, :], rs[:, b:b + 1], x[:, b, :],
                                             ALU.mult, ALU.add).then_inc((x_first, x_ready)[b], 1)

            def ffn(f, name):
                norm_in(name)
                base, done = AT[name], FC * f
                hid = region(ARENA, 2, 2, T)[0]

                def hidden(c, i=None):
                    up, silu = ps[:, 4 + c % 2, T:2 * T], hid[:, 0, c % 2, :]
                    dve.tensor_tensor(w_hi[:, c % 2, :], up, silu, ALU.mult)
                    dve.tensor_tensor(hid[:, 1, c % 2, :], up, silu, ALU.mult).then_inc(of("product"), 1)
                    dve.wait_ge(of("product"), count(done + c + 1, i, 4))
                    dve.tensor_tensor(w_lo[:, c % 2, :], hid[:, 1, c % 2, :], w_hi[:, c % 2, :].bitcast(F32),
                                      ALU.subtract).then_inc(hidden_ready, 1)

                dve.wait_ge(silu_ready, done + 1)
                hidden(0)
                make_lo(dve, base + 4)
                make_lo(dve, base + 5)
                dve.wait_ge(silu_ready, done + 2)
                hidden(1)
                with dve.Fori(0, 5) as i:
                    for j in range(4):
                        c = 2 + j
                        for b in range(3 * c, 3 * c + 3):
                            make_lo(dve, base + b, i, 12)
                        dve.wait_ge(silu_ready, i * 4 + (done + c + 1))
                        dve.wait_ge(used, i * 12 + (base + 3 * c - 1))
                        hidden(c, i)
                add_normed(0.5)

            def stick_breaking():
                norm_in("sb")
                own_wait("sb")
                base = AT["sb_qkv"]
                R = sb_regions()
                pairs = HEADS // 2

                def evac(j):
                    if j >= 2:
                        dve.wait_ge(of("sb_av"), j - 1)
                    dve.wait_ge(used, base + 3 * j + 3)
                    dve.tensor_copy(R["v"][:, j % 2], ps[:, 2 + j % 2, 0:T].rearrange("p (a b) -> p a b", a=TB))\
                       .then_inc(of("sb_v"), 1)

                evac(0)
                for j in range(pairs):
                    dve.wait_ge(of("sb_l"), j + 1)
                    dve.tensor_copy(R["z"][:, :, :], ps[:, 4:6, 0:384])
                    dve.wait_ge(of("sb_r"), j) if j else None
                    link(dve.scalar_tensor_tensor(R["sp"][:, :, 0:384], ps[:, 4:6, 0:384], 0.0,
                                                  R["lz"][:, :, :], ALU.max, ALU.add))
                    for e in range(2):
                        diag = R["sp"][:, e].rearrange("p (a b) -> p a b", a=2)[:, :, 0:P]
                        last = dve.tensor_tensor(diag, diag, R["own"][:, 0, :].unsqueeze(1)
                                                 .to_broadcast([P, 2, P]), ALU.mult)
                    last.then_inc(of("sb_sp"), 1)
                    dve.wait_ge(of("sb_r"), j + 1)
                    dve.wait_ge(of("sb_a"), j) if j else None
                    link(dve.tensor_tensor(R["t"][:, :, :], R["z"][:, :, :], ps[:, 6:8, 0:384], ALU.subtract))
                    for e in range(2):
                        for s in range(2):
                            diag = R["t"][:, e, s * T:s * T + P]
                            last = dve.tensor_tensor(diag, diag, R["own"][:, 1, :], ALU.add)
                    last.then_inc(of("sb_t"), 1)
                    if j + 1 < pairs:
                        evac(j + 1)
                    dve.wait_ge(of("sb_av"), j + 1)
                    dve.tensor_copy(R["oT"][:, j, :], ps[:, 4, 0:T]).then_inc(of("sb_o"), 1)
                add_normed(1.0)

            def add(*sources):
                for b in range(TB):
                    y = bank(2 * b, 2)
                    if sources:
                        link(dve.tensor_tensor(xn[:, b, :], y, sources[0], ALU.add))
                        y = xn[:, b, :]
                    dve.tensor_tensor(x[:, b, :], x[:, b, :], y, ALU.add).then_inc((x_first, x_ready)[b], 1)

            def rotate(v, n, half, tb, at, tmp):
                c = cosT[:, tb, at:at + half].unsqueeze(1).to_broadcast([P, n, half])
                s_ = sinT[:, tb, at:at + half].unsqueeze(1).to_broadcast([P, n, half])
                t = [tmp[:, k, 0:n * half].rearrange("p (n h) -> p n h", n=n) for k in range(4)]
                x1, x2 = v[:, :, 0:half], v[:, :, half:2 * half]
                dve.tensor_tensor(t[0], x1, c, ALU.mult)
                dve.tensor_tensor(t[1], x2, s_, ALU.mult)
                dve.tensor_tensor(t[2], x2, c, ALU.mult)
                link(dve.tensor_tensor(t[3], x1, s_, ALU.mult))
                dve.tensor_tensor(x1, t[0], t[1], ALU.subtract)
                link(dve.tensor_tensor(x2, t[2], t[3], ALU.add))

            def angles():
                TWO_PI, MAGIC = 2 * np.pi, 1.5 * 2.0 ** 23
                c1 = 6.28125
                c2 = float(np.float32(np.round((TWO_PI - c1) * 2.0 ** 22) / 2.0 ** 22))
                c3 = float(np.float32(TWO_PI - c1 - c2))
                inv = col("inv")
                a = [ang[:, k].rearrange("p a b -> p (a b)") for k in range(4)]
                link(dve.tensor_copy(posf[:, :], pos[:, :]))
                for w, (lo, hi) in enumerate(((0, 16), (16, 24))):
                    for tb in range(TB):
                        last = dve.tensor_scalar(ang[:, 0, tb, lo:hi], inv[:, lo:hi],
                                                 posf[:, w * TB + tb:w * TB + tb + 1], None, ALU.mult)
                link(last)
                link(dve.tensor_scalar(a[1], a[0], float(1 / TWO_PI), MAGIC, ALU.mult, ALU.add))
                link(dve.tensor_scalar(a[2], a[1], MAGIC, None, ALU.subtract))
                for c in (c1, c2, c3):
                    link(dve.scalar_tensor_tensor(a[0], a[2], -c, a[0], ALU.mult, ALU.add))
                dve.tensor_scalar(a[1], a[0], 3.1415925, -3.1415925, ALU.min, ALU.max).then_inc(of("angle"), 1)
                dve.wait_ge(of("angle_abs"), 1)
                dve.tensor_scalar(a[3], a[2], -1.0, float(np.pi / 2), ALU.mult, ALU.add).then_inc(of("angle"), 1)
                dve.wait_ge(of("angle_sin"), 1)

            def attention(a, R):
                pairs, n0 = HEADS // 2, a * (HEADS // 2)
                scale = float(QD) ** -0.5 if a == 0 else 0.125
                own_wait("swa" if a else "mla")
                neg = R["own"].unsqueeze(1).to_broadcast([P, 2, 384])

                def masked(j):
                    dve.wait_ge(of("att_s"), n0 + j + 1)
                    if j >= 2:
                        dve.wait_ge(of("att_p"), n0 + j - 1)
                    st, nm = R["st"][:, j % 2], R["nm"][:, j % 2].rearrange("p (e t) -> p e t", e=2)
                    link(dve.scalar_tensor_tensor(st, ps[:, 2:4, 0:384], scale, neg, ALU.mult, ALU.add))
                    dve.tensor_reduce(nm[:, :, 0:1], st[:, :, 0:P], AX.X, ALU.max, negate=True)
                    last = dve.tensor_reduce(nm[:, :, 1:2], st[:, :, P:384], AX.X, ALU.max, negate=True)
                    if a:
                        link(last)
                        sink = R["nsink"][:, 2 * j:2 * j + 2].unsqueeze(2).to_broadcast([P, 2, 2])
                        last = dve.tensor_tensor(nm, nm, sink, ALU.min)
                    last.then_inc(of("att_m"), 1)

                def normed(j):
                    dve.wait_ge(of("att_p"), n0 + j + 1)
                    su, p = R["su"][:, j % 2], R["p"][:, j % 2]
                    if a:
                        link(dve.tensor_tensor(su, su, R["es"][:, j % 2], ALU.add))
                    link(dve.reciprocal(R["rc"], su))
                    rc = R["rc"].rearrange("p (e t) -> p e t", e=2)
                    dve.tensor_tensor(p[:, :, 0:P], p[:, :, 0:P], rc[:, :, 0:1].to_broadcast([P, 2, P]), ALU.mult)
                    dve.tensor_tensor(p[:, :, P:384], p[:, :, P:384], rc[:, :, 1:2].to_broadcast([P, 2, T]),
                                      ALU.mult).then_inc(of("att_n"), 1)

                masked(0)
                for j in range(pairs):
                    if j + 1 < pairs:
                        masked(j + 1)
                    normed(j)
                    dve.wait_ge(of("att_av"), n0 + j + 1)
                    dve.tensor_copy(R["oT"][:, j, :], ps[:, 6 + j % 2, 0:T]).then_inc(of("att_o"), 1)

            def mla():
                norm_in("mla")
                R = attention_regions(0)
                rstd([(0, 2, 1.0 / QL, EPS), (2, 4, 1.0 / KVL, EPS)])
                for tb in range(TB):
                    dve.tensor_scalar(R["cn"][:, tb, 0:QL], R["mp"][:, tb, 0:QL], rs[:, tb:tb + 1], None, ALU.mult)
                    last = dve.tensor_scalar(R["cn"][:, tb, QL:QL + KVL], R["mp"][:, tb, QL:QL + KVL],
                                             rs[:, 2 + tb:3 + tb], None, ALU.mult)
                last.then_inc(of("mla_cn"), 1)
                for tb in range(TB):
                    kr = R["mp"][:, tb, QL + KVL:MLA_IN].unsqueeze(1)
                    rotate(kr, 1, 16, tb, 0, R["rot"])
                    dve.tensor_copy(split(R["k"][:, tb, :], HEADS, QD)[:, :, 64:QD], kr.to_broadcast([P, HEADS, ROPE]))
                dve.wait_ge(of("mla_q"), 1)
                for tb in range(TB):
                    rotate(split(R["q"][:, tb, :], HEADS, QD)[:, :, 64:QD], HEADS, 16, tb, 0, R["rot"])
                dve.wait_ge(used, AT["mla_ukv"] + 2)
                kv = bank(4, 4).rearrange("p (h c) -> p h c", h=HEADS)
                dve.tensor_copy(split(R["k"][:, 1, :], HEADS, QD)[:, :, 0:64], kv[:, :, 0:64])
                dve.tensor_copy(split(R["v"][:, 1, :], HEADS, 64), kv[:, :, 64:128]).then_inc(of("mla_kv_d"), 1)
                attention(0, R)
                add_normed(1.0)

            def swa():
                R = attention_regions(1)
                norm_in("kv")
                dve.wait_ge(used, AT["swa_kv"] + 2)
                for tb in range(TB):
                    last = dve.tensor_tensor(R["kv"][:, tb, :], ps[:, 4 + tb, 0:256], col("kv_b"), ALU.add)
                link(last)
                for tb in range(TB):
                    rotate(split(R["kv"][:, tb, 0:P], 2, 64)[:, :, 0:ROT], 2, ROT // 2, tb, 16, R["rot"])
                dve.tensor_scalar(R["nsink"], col("sinks"), -1.0, None, ALU.mult)
                for tb in range(TB):
                    for g in range(2):
                        last = dve.tensor_copy(split(R["kd"][:, tb, g, :], 2, 64),
                                               R["kv"][:, tb, g * 64:g * 64 + 64].unsqueeze(1).to_broadcast([P, 2, 64]))
                last.then_inc(of("swa_k"), 1)
                norm_in("swa")
                dve.wait_ge(used, AT["swa_q"] + KD)
                row_wait(0)
                for tb in range(TB):
                    last = dve.tensor_tensor(R["q"][:, tb, :], bank(2 * tb, 2), row[:, 0, :], ALU.add)
                link(last)
                for tb in range(TB):
                    rotate(split(R["q"][:, tb, :], HEADS, 64)[:, :, 0:ROT], HEADS, ROT // 2, tb, 16, R["rot"])
                link(dve.tensor_copy(R["rc"], R["nsink"][:, 0:4]))
                dve.tensor_copy(R["rc"], R["nsink"][:, 0:4]).then_inc(of("swa_q"), 1)
                attention(1, R)
                dve.wait_ge(used, AT["swa_out"] + KD)
                row_wait(1)
                add(row[:, 1, :])

            def ssm():
                R = ssm_regions()
                norm_in("ssm")
                own_wait("ssm")
                conv = CAT["conv"][0]
                with dve.Fori(0, CONV_TILES // 4) as i:
                    for j in range(4):
                        dve.wait_ge(of("conv_acc"), i * 4 + (j + 1))
                        for k in range(3):
                            if k:
                                dve.wait_ge(of("conv_taps"), i * 12 + (3 * j + k))
                            d = k + 1
                            dve.scalar_tensor_tensor(R["acc"][:, j, d:T], ps[:, j, 0:T - d],
                                                     cols[:, bass.ds(i * 20 + (conv + 5 * j + 2 - k), 1)],
                                                     R["acc"][:, j, d:T], ALU.mult, ALU.add)\
                               .then_inc(of("conv_taps"), 1)
                two = [P, TB, SH]

                def heads(v):
                    return v.rearrange("p (c h) -> p c h", c=TB)

                dve.wait_ge(used, AT["ssm_dt"] + 1)
                dve.tensor_tensor(heads(R["u"]), heads(ps[:, 4, 0:64]), col("dt_bias").unsqueeze(1).to_broadcast(two),
                                  ALU.add).then_inc(of("ssm_u"), 1)
                dve.wait_ge(of("ssm_l"), 1)
                link(dve.scalar_tensor_tensor(R["dt"], R["u"], 0.0, R["lz"], ALU.max, ALU.add))
                dve.scalar_tensor_tensor(heads(R["a"]), heads(R["dt"]), -1.0,
                                         R["eA"].unsqueeze(1).to_broadcast(two), ALU.mult, ALU.mult)\
                   .then_inc(of("ssm_a"), 1)
                dve.wait_ge(of("ssm_cs"), 1)
                link(dve.tensor_copy(R["acs"], ps[:, 5, 0:64]))
                dve.tensor_tensor(R["de"], ps[:, 5, 64:128], R["acs"], ALU.subtract).then_inc(of("ssm_de"), 1)
                for n in range(8):
                    dve.wait_ge(of("ssm_xs"), n + 1)
                    tb, m = n % 2, n // 2
                    last = dve.tensor_tensor(split(R["X"][:, tb, m * 512:(m + 1) * 512], 8, 64),
                                             split(R["xs"][:, tb, m * 512:(m + 1) * 512], 8, 64),
                                             R["dt"][:, tb * SH + 8 * m:tb * SH + 8 * m + 8].unsqueeze(2)
                                             .to_broadcast([P, 8, 64]), ALU.mult)
                link(last)
                dve.wait_ge(of("ssm_ex"), 1)

                def per_head(v, c, g):
                    o = c * SH + HPG * g
                    return v[:, o:o + HPG].unsqueeze(2).to_broadcast([P, HPG, 64])

                def spread(n):
                    g, c = n // 2, n % 2
                    if n >= 2:
                        dve.wait_ge(of("sg_cb"), n - 1)
                    o = c * SH + HPG * g
                    dve.tensor_tensor(R["ta"][:, n % 2], col("up_incl").unsqueeze(1).to_broadcast([P, HPG, P]),
                                      R["a"][:, o:o + HPG].unsqueeze(2).to_broadcast([P, HPG, P]), ALU.mult)\
                       .then_inc(of("sg_ta"), 1)

                def outputs(n):
                    g, c = n // 2, n % 2
                    o = slice(g * T, (g + 1) * T)
                    t = R["t"]
                    if n:
                        dve.wait_ge(of("sg_done"), n)
                    link(dve.tensor_tensor(split(t[:, 0], HPG, 64), split(R["xs"][:, c, o], HPG, 64),
                                           col("d_skip")[:, HPG * g:HPG * g + HPG].unsqueeze(2)
                                           .to_broadcast([P, HPG, 64]), ALU.mult))
                    dve.wait_ge(of("sg_y"), n + 1)
                    if c:
                        link(dve.tensor_tensor(split(t[:, 1], HPG, 64), split(ps[:, 4 + n % 2, T:2 * T], HPG, 64),
                                               per_head(R["eacs"], c, g), ALU.mult))
                        link(dve.tensor_tensor(t[:, 0], t[:, 0], t[:, 1], ALU.add))
                    dve.tensor_tensor(t[:, 0], t[:, 0], ps[:, 4 + n % 2, 0:T], ALU.add).then_inc(of("sg_o"), 1)
                    dve.wait_ge(of("sg_o"), n + 1)
                    dve.tensor_tensor(R["zs"][:, c, o], R["zs"][:, c, o], t[:, 0], ALU.mult)\
                       .then_inc(of("sg_done"), 1)

                spread(0)
                for n in range(2 * SG):
                    g, c = n // 2, n % 2
                    if n + 1 < 2 * SG:
                        spread(n + 1)
                    dve.wait_ge(of("sg_cb"), n + 1)
                    if n >= 2:
                        dve.wait_ge(of("sg_L"), n - 1)
                    for q in range(HPG):
                        o = c * SH + HPG * g + q
                        last = dve.scalar_tensor_tensor(R["seg"][:, n % 2, q, :], ps[:, n % 2, q * P:(q + 1) * P],
                                                        R["acs"][:, o:o + 1], R["own"],
                                                        ALU.subtract, ALU.add)
                    last.then_inc(of("sg_seg"), 1)
                    if n:
                        outputs(n - 1)
                    if n >= 2:
                        dve.wait_ge(of("sg_y"), n - 1)
                    if c == 0:
                        link(dve.tensor_tensor(split(R["Xd"][:, g % 2, :], HPG, 64),
                                               split(R["X"][:, 0, g * T:(g + 1) * T], HPG, 64),
                                               per_head(R["dte"], 0, g), ALU.mult))
                    dve.wait_ge(of("sg_L"), n + 1)
                    dve.tensor_tensor(R["M"][:, n % 2], R["L"][:, n % 2],
                                      ps[:, 2 + n % 2, 0:P].unsqueeze(1).to_broadcast([P, HPG, P]), ALU.mult)\
                       .then_inc(of("sg_M"), 1)
                outputs(2 * SG - 1)
                rstd([(0, 16, 1.0 / T, 1e-5)])
                for tb in range(TB):
                    v = split(R["zs"][:, tb, :], SG, T)
                    dve.tensor_tensor(v, v, rs[:, tb * SG:(tb + 1) * SG].unsqueeze(2).to_broadcast([P, SG, T]),
                                      ALU.mult).then_inc(of("ssm_yn"), 1)
                for k in (2, 3, 6, 7, 10, 11, 14, 15):
                    dve.wait_ge(of("ssm_yT"), k // 2 + 1)
                    dve.tensor_scalar(R["yT"][:, k, :], ps[:, k // 2, (k % 2) * T:(k % 2 + 1) * T],
                                      col("gate_norm")[:, k:k + 1], None, ALU.mult).then_inc(of("ssm_yT_d"), 1)
                dve.wait_ge(used, AT["ssm_out"] + DI // P)
                add()

            def top16(src, spare, values, indices):
                both = range(TB)
                for b in both:
                    last = dve.max(values(b, 0), src(b))
                link(last)
                for b in both:
                    dve.max_index(indices(b, 0), values(b, 0), src(b))
                    last = dve.match_replace(spare(b), values(b, 0), src(b), -3.0e38)
                link(last)
                for b in both:
                    last = dve.max(values(b, 8), spare(b))
                link(last)
                for b in both:
                    last = dve.max_index(indices(b, 8), values(b, 8), spare(b))
                return last

            def peer(l):
                R = peer_regions()
                norm_in(f"peer{l}")
                n0 = SUBS * l
                si = R["si"].bitcast(U32)
                for m in range(SUBS):
                    dve.wait_ge(of("peer_sp"), n0 + m + 1)
                    dve.tensor_copy(R["s"][:, :, m, :], ps[:, 2 + m % 2, 0:T].rearrange("p (b k) -> p b k", b=TB))\
                       .then_inc(of("peer_s"), 1)
                    dve.wait_ge(of("peer_s"), n0 + m + 1)
                    link(top16(lambda b: R["s"][:, b, m, :], lambda b: R["s2"][:, b, :],
                               lambda b, o: R["sv"][:, b, m, o:o + 8], lambda b, o: si[:, b, m, o:o + 8]))
                link(dve.tensor_copy(R["sif"], si))
                bp = R["bp"].bitcast(U32)
                bp3 = bp.rearrange("p (b h k) -> p b h k", b=TB, h=PH)
                for h in range(PH):
                    for b in range(TB):
                        last = dve.tensor_tensor(split(R["cand"][:, b, :], TOPK, TOPK),
                                                 R["sv"][:, b, 2 * h, :].unsqueeze(2).to_broadcast([P, TOPK, TOPK]),
                                                 R["sv"][:, b, 2 * h + 1, :].unsqueeze(1).to_broadcast([P, TOPK, TOPK]),
                                                 ALU.add)
                    link(last)
                    link(top16(lambda b: R["cand"][:, b, :], lambda b: R["cand2"][:, b, :],
                               lambda b, o: R["bs"][:, b, h, o:o + 8], lambda b, o: bp3[:, b, h, o:o + 8]))
                n = TB * PH
                bs3 = R["bs"].rearrange("p b h k -> p (b h) k")
                e3 = R["e"].rearrange("p b h k -> p (b h) k")
                dve.tensor_tensor(e3, bs3, bs3[:, :, 0:1].to_broadcast([P, n, TOPK]), ALU.subtract)\
                   .then_inc(of("peer_e"), 1)
                pa = R["pa"].bitcast(U32)
                dve.tensor_scalar(pa[:, 0, :], bp, 4, None, ALU.logical_shift_right)
                link(dve.tensor_scalar(pa[:, 1, :], bp, 15, None, ALU.bitwise_and))
                link(dve.tensor_copy(R["pf"].rearrange("p c b h k -> p c (b h k)"), pa))
                full = [P, PH, TOPK, TOPK]
                iota = col("iota")[:, 0:TOPK].unsqueeze(1).unsqueeze(1).to_broadcast(full)
                for b in range(TB):
                    keys = R["sif"][:, b].rearrange("p (h c) a -> p h c a", c=2)
                    for c in range(2):
                        link(dve.tensor_tensor(R["eq"], R["pf"][:, c, b].unsqueeze(3).to_broadcast(full), iota,
                                               ALU.is_equal))
                        link(dve.tensor_tensor(R["eq"], R["eq"], keys[:, :, c, :].unsqueeze(2).to_broadcast(full),
                                               ALU.mult))
                        link(dve.tensor_reduce(split(R["pk"][:, c, b, :], PH, TOPK).unsqueeze(3), R["eq"], AX.X,
                                               ALU.add))
                dve.wait_ge(of("peer_ex"), l + 1)
                link(dve.tensor_reduce(R["sum"].unsqueeze(2), e3, AX.X, ALU.add))
                link(dve.reciprocal(R["rc"], R["sum"]))
                dve.tensor_tensor(R["pk"][:, 2].rearrange("p b (h k) -> p (b h) k", h=PH), e3,
                                  R["rc"].unsqueeze(2).to_broadcast([P, n, TOPK]), ALU.mult).then_inc(of("picks"), 1)
                n0 = 64 * l
                dve.wait_ge(of("picksTs"), l + 1)
                dve.wait_ge(of("gelu"), n0 + 64)
                def hot(n, i=None):
                    t = 4 * n if i is None else i * 16 + 4 * n
                    if n >= 2:
                        g = n0 + n - 1
                        dve.wait_ge(of("gates"), g if i is None else i * 4 + g)
                    for q in range(4):
                        key1, key2, gate = (pick[:, c, bass.ds(t + q, 1)] for c in range(3))
                        if q < HOT_BY_DVE:
                            dve.tensor_scalar(R["hot"][:, n % 2, 0, q], col("iota"), key1, None, ALU.is_equal)
                        last = dve.tensor_scalar(R["hot"][:, n % 2, 1, q], col("iota"), key2, gate, ALU.is_equal,
                                                 ALU.mult)
                    last.then_inc(of("hot"), 1)

                def gated(n, i=None):
                    t = 4 * n if i is None else i * 16 + 4 * n
                    g = n0 + n + 1
                    dve.wait_ge(of("gates"), g if i is None else i * 4 + g)
                    w = R["A"][:, :, bass.ds(t, 4)].rearrange("p i t -> p t i")
                    dve.tensor_tensor(w, w, ps[:, n % 4, :].rearrange("p (t i) -> p t i", t=4), ALU.mult)\
                       .then_inc(of("gated"), 1)

                hot(0)
                hot(1)
                gated(0)
                hot(2)
                gated(1)
                with dve.Fori(0, 15) as i:
                    for n in range(3, 7):
                        hot(n, i)
                        gated(n - 1, i)
                hot(63)
                gated(62)
                gated(63)
                base, n0 = AT[f"peer{l}_v"], KEYS * l

                def rests(js, i=None):
                    for j in js:
                        dve.wait_ge(of("peer_wh"), count(n0 + j + 1, i, 4))
                        dve.tensor_tensor(w_lo[:, j % 2, :], gated_tile(R, j, i), w_hi[:, j % 2, :].bitcast(F32),
                                          ALU.subtract).then_inc(of("peer_w"), 1)
                        if 2 <= j < KEYS - 2:
                            make_lo(dve, base + j + 2, i, 4)

                rests(range(4))
                with dve.Fori(0, KEYS // 4 - 2) as i:
                    rests(range(4, 8), i)
                rests(range(KEYS - 4, KEYS))
                dve.wait_ge(used, AT[f"peer{l}_v"] + KEYS)
                add()

            def ple(l):
                norm_in(f"ple{l}")
                sg = region(ARENA + 2 * T, TB, D)[0]
                dve.wait_ge(of("ple_gate"), l + 1)
                dve.wait_ge(used, AT[f"ple{l}_proj"] + 2)
                for b in range(TB):
                    link(dve.tensor_tensor(xn[:, b, :], sg[:, b, :], bank(4 + 2 * b, 2), ALU.mult))
                    dve.tensor_tensor(x[:, b, :], x[:, b, :], xn[:, b, :], ALU.add)\
                       .then_inc((x_first, x_ready)[b], 1)


            link(dve.memset(ms[:, :], 1.0))
            dve.wait_ge(pos_loaded, 16)
            dve.wait_ge(cols_loaded, 16)
            dve.wait_ge(x_loaded, 16)
            angles()
            fs = 0
            for name in LAYERS:
                if name.startswith("ffn"):
                    ffn(fs, name)
                    fs += 1
                elif name == "sb":
                    stick_breaking()
                elif name in ("mla", "swa", "ssm"):
                    {"mla": mla, "swa": swa, "ssm": ssm}[name]()
                elif name.startswith("peer"):
                    peer(int(name[-1]))
                elif name.startswith("ple"):
                    ple(int(name[-1]))
            rstd([(0, TB, 1.0 / D, EPS)])
            row_wait(0)
            for b in range(TB):
                dve.scalar_tensor_tensor(xn[:, b, :], x[:, b, :], rs[:, b:b + 1], row[:, 0, :],
                                         ALU.mult, ALU.mult).then_inc(of("result"), 1)
            n_stats[0] = stats[0]

        @block.gpsimd
        def _(pool):
            pool.wait_ge(cols_loaded, 16)

            def powers(first, end):
                if first == end:
                    return
                with pool.Fori(0, end - first) as i:
                    pool.wait_ge(ms_ready, i + (first + 1))
                    pool.tensor_tensor(rs[:, :], ms[:, :], col("nhalf"), ALU.pow).then_inc(rs_ready, 1)

            def lows(first, end):
                turns = (end - first) // SLOTS if end - first > SLOTS else 0
                if turns:
                    with pool.Fori(0, turns) as i:
                        for b in range(SLOTS):
                            make_lo(pool, first + b, i, SLOTS)
                for b in range(first + turns * SLOTS, end):
                    make_lo(pool, b)

            at = 0
            for name, n in stats_before.items():
                powers(at, n)
                first = AT[FIRST_PART[name]]
                for b in range(2):
                    make_lo(pool, first + b)
                powers(n, n + 1)
                at = n + 1
                lows(first + 2, first + POOL_BLOCKS[name])
            powers(at, n_stats[0])


def by_rows(w):
    return w.reshape(-1, P, w.shape[-1])


def by_columns(w):
    return w.reshape(KD, P, -1, P).transpose(2, 1, 0, 3).reshape(-1, P, KD * P)


def padded(w):
    full = np.zeros((w.shape[0], P, BLK), w.dtype)
    full[:, :, :w.shape[2]] = w
    return full


def grouped(w, n):
    c = w.shape[1]
    w = w.reshape(-1, n, P, c).transpose(0, 2, 1, 3)
    return w.reshape(-1, P, n * c)


def feed_forward(w_in, w_out):
    cols, down = by_columns(w_in), by_rows(w_out)
    gate, up = cols[:FC], cols[FC:]
    out = [gate[0:1], up[0:1]]
    both = np.stack([gate[1:], up[1:], down[:-1]], 1).reshape(-1, P, BLK)
    return out + [both, down[-1:]]


def weight_stream(a):
    ffn = [feed_forward(a["ffn_w_in"][i, j], a["ffn_w_out"][i, j]) for i in range(2) for j in range(2)]
    qkv = by_columns(a["sb_w_in"][0]).reshape(3, KD, P, BLK).transpose(1, 0, 2, 3).reshape(-1, P, BLK)
    uq = a["mla_w_uq"][0].reshape(2, P, 3, 512).transpose(2, 1, 0, 3).reshape(3, P, BLK)
    ukv = a["mla_w_ukv"][0].reshape(P, 2, BLK).transpose(1, 0, 2)
    ssm = a["ssm_in_w_2"][0]
    z = ssm[:, :DI].reshape(KD, P, 2, D).transpose(2, 0, 1, 3).reshape(16, P, D)

    def peer(i):
        u = a["peer_u_2"][i].reshape(KEYS, KEYS, KD, P).transpose(1, 3, 2, 0).reshape(KEYS, P, BLK)
        v = a["peer_v_2"][i].reshape(KEYS, KEYS, D).transpose(1, 0, 2)
        return [by_columns(a["peer_q_w_2"][i]), u, v, by_rows(a["ple_gate_w_2"][i]), by_rows(a["ple_proj_2"][i])]

    parts = ffn[0] + [qkv, by_rows(a["sb_w_out"][0])] + ffn[1] + ffn[2]
    parts += [padded(grouped(a["mla_w_in"][0], 2)), uq, ukv, by_rows(a["mla_w_out"][0])] + ffn[3]
    parts += [z, by_columns(ssm[:, DI:DI + CONV_TILES * P]), padded(grouped(ssm[:, DI + CONV_TILES * P:], KD)),
              by_rows(a["ssm_out_w_2"][0])]
    parts += peer(0) + [grouped(a["kv_w_2"], 4), by_rows(a["q_w_2"][0]), by_rows(a["o_w_2"][0])] + peer(1)
    return np.concatenate(parts)


def columns(a):
    i, j = np.arange(P)[:, None], np.arange(P)[None, :]
    f = np.float32

    def tall(v):
        return np.asarray(v).reshape(-1, P).T

    def wide(v):
        return np.broadcast_to(np.asarray(v).reshape(1, -1), (P, np.asarray(v).size))

    neg = f(NEG)
    causal = np.where(j <= i, f(0), neg)
    after = np.where(i <= j, f(0), neg)
    inv1 = np.power(10000.0, (-np.arange(0, ROPE, 2, dtype=f) / f(ROPE)).astype(np.float64)).astype(f)
    inv2 = np.power(500000.0, (-np.arange(0, ROT, 2, dtype=f) / f(ROT)).astype(np.float64)).astype(f)
    g, ng = a["norm_g"], np.concatenate
    gains = [g[0, 0], g[0, 2], g[0, 4], g[1, 0], g[1, 2], g[1, 4], a["ssm_norm_2"][0], a["peer_norm_2"][0],
             a["ple_norm_2"][0], a["kv_norm_2"], a["attn_norm_2"][0], a["peer_norm_2"][1], a["ple_norm_2"][1]]
    conv = ng([a["ssm_conv_w_2"][0], a["ssm_conv_b_2"]]).reshape(5, CONV_TILES, P).transpose(2, 1, 0)
    subkeys = a["peer_sub_keys_2"].transpose(3, 0, 1, 2).reshape(P, -1)
    pT = a["p_2"].reshape(2, T, 2, P).transpose(3, 0, 2, 1).reshape(P, 2, -1)
    parts = {"ident": i == j, "up_incl": i <= j, "lo_incl": i >= j, "up_strict": i < j,
             "neg_strict": np.where(i < j, f(0), neg), "neg_causal": ng([causal, np.zeros((P, P), f), causal], 1),
             "neg_window": ng([causal, np.where(j > i, f(0), neg), causal], 1), "neg_after": after,
             "ones": np.ones((P, P)), "iota": wide(np.arange(P)), "inv": wide(ng([inv1, inv2])),
             "nhalf": np.full((P, 16), -0.5), "gains": ng([tall(v) for v in gains], 1),
             "gate_norm": tall(a["ssm_gate_norm_2"]), "q_norm": tall(a["mla_q_norm"]),
             "kv_norm": tall(a["mla_kv_norm"]), "conv": conv.reshape(P, -1), "subkeys": subkeys,
             "dt_bias": wide(a["ssm_dt_bias_2"]), "a_log": wide(a["ssm_A_log_2"]), "d_skip": wide(a["ssm_D_2"]),
             "sinks": wide(a["sinks_2"]), "kv_b": wide(a["kv_b_2"]), "pT0": pT[:, 0], "pT1": pT[:, 1]}
    return ng([np.asarray(parts[name], f) for name, _ in COLS + OWN_COLS], 1)


def laid_out(inputs):
    a = {k: np.asarray(v) for k, v in inputs.items()}
    g = a["norm_g"]
    pos = np.stack([a["positions"][0].reshape(TB, P), a["positions_2"][0].reshape(TB, P)]).transpose(2, 0, 1)
    rows = np.stack([g[0, 1], g[0, 3], g[0, 5], g[1, 1], g[1, 3], g[1, 5], a["q_b_2"][0], a["final_norm_2"],
                     a["o_b_2"][0]])
    return {"stream": weight_stream(a), "x_in": np.ascontiguousarray(a["x"][0]),
            "pos_in": np.ascontiguousarray(pos.reshape(P, 2 * TB).astype(np.int32)),
            "cols_in": np.ascontiguousarray(columns(a)), "rows_in": rows}


def kernel(**inputs):
    import concourse.bacc as bacc
    from concourse.bass_utils import run_bass_kernel_spmd

    arrays = laid_out(inputs)
    nc = bacc.Bacc("TRN2", target_bir_lowering=False, num_devices=1, dynamic_dma_scratch_size=256)
    args = [nc.dram_tensor(name, a.shape, mybir.dt.from_np(a.dtype), kind="ExternalInput").ap()
            for name, a in arrays.items()]
    out = nc.dram_tensor("out", (T, D), F32, kind="ExternalOutput").ap()
    build_program(nc, *args, out)
    r = run_bass_kernel_spmd(nc, [arrays], core_ids=[0])
    return r.results[0]["out"].reshape(1, T, D)
```
